# Optimizing a Trainium2 kernel written in Bass

```python
import jax, jax.numpy as jnp
from jax import lax
import numpy as np

D_MODEL = 1024
BATCH = 1
SEQ = 256
DEPTH = 2

N_HEADS = 8
N_KV_HEADS = 2
HEAD_DIM = 128
Q_GROUP = N_HEADS // N_KV_HEADS
WINDOW = 128
BLOCK = 128
ROPE_THETA = 500000.0
ROPE_DIM = HEAD_DIM // 4
D_RNN = D_MODEL
N_RNN_BLOCKS = 4
RNN_BLOCK_W = D_RNN // N_RNN_BLOCKS
RNN_CONV_W = 4
RG_C = 8.0
D_FF = 3 * D_MODEL
FFN_CONV_W = 3
D_PLE = 256
LN_EPS = 1e-5
DN_ALPHA = (2 * DEPTH) ** 0.25
DN_BETA = (8 * DEPTH) ** -0.25

Q_WIDTH = N_HEADS * HEAD_DIM
KV_WIDTH = N_KV_HEADS * HEAD_DIM
IN_SIZES = (Q_WIDTH, KV_WIDTH, KV_WIDTH, D_RNN, D_RNN, D_MODEL, D_MODEL)
D_IN = sum(IN_SIZES)

kernel_name = "hybrid_swa_rglru_bidir_encoder"

def layer_norm(x, g, b):
    xf = x.astype(jnp.float32)
    mu = jnp.mean(xf, axis=-1, keepdims=True)
    var = jnp.mean(jnp.square(xf - mu), axis=-1, keepdims=True)
    y = (xf - mu) * lax.rsqrt(var + LN_EPS) * g.astype(jnp.float32) + b.astype(jnp.float32)
    return y.astype(x.dtype)

def rope_tables(seq_len, dtype):
    pos = jnp.arange(seq_len, dtype=jnp.float32)
    inv = ROPE_THETA ** (-jnp.arange(0, ROPE_DIM, 2, dtype=jnp.float32) / ROPE_DIM)
    ang = pos[:, None] * inv[None, :]
    return jnp.cos(ang).astype(dtype), jnp.sin(ang).astype(dtype)

def partial_rope(x, cos, sin):
    half = ROPE_DIM // 2
    x1, x2, rest = x[..., :half], x[..., half:ROPE_DIM], x[..., ROPE_DIM:]
    c = cos[None, :, None, :]
    s = sin[None, :, None, :]
    return jnp.concatenate([x1 * c - x2 * s, x2 * c + x1 * s, rest], axis=-1)

def band_blocks(t):
    bsz, s = t.shape[:2]
    nb = s // BLOCK
    tp = jnp.pad(t, ((0, 0), (BLOCK, BLOCK), (0, 0), (0, 0)))
    tb = tp.reshape(bsz, nb + 2, BLOCK, *t.shape[2:])
    return jnp.concatenate([tb[:, :-2], tb[:, 1:-1], tb[:, 2:]], axis=2)

def local_attention(q, k, v, sink):
    bsz, s = q.shape[:2]
    nb = s // BLOCK
    qb = q.reshape(bsz, nb, BLOCK, N_KV_HEADS, Q_GROUP, HEAD_DIM)
    kb = band_blocks(k)
    vb = band_blocks(v)
    logits = jnp.einsum('bnqhgd,bnkhd->bnhgqk', qb, kb,
                        preferred_element_type=jnp.float32) * (HEAD_DIM ** -0.5)
    qi = jnp.arange(BLOCK)[:, None]
    kj = jnp.arange(3 * BLOCK)[None, :]
    band = jnp.abs(kj - BLOCK - qi) <= WINDOW
    kpos = jnp.arange(nb)[:, None] * BLOCK - BLOCK + jnp.arange(3 * BLOCK)[None, :]
    in_range = (kpos >= 0) & (kpos < s)
    valid = band[None] & in_range[:, None, :]
    logits = jnp.where(valid[None, :, None, None], logits, -1e30)
    sink_col = jnp.broadcast_to(
        sink.astype(jnp.float32).reshape(1, 1, N_KV_HEADS, Q_GROUP, 1, 1),
        logits.shape[:-1] + (1,))
    probs = jax.nn.softmax(jnp.concatenate([logits, sink_col], axis=-1), axis=-1)[..., :-1]
    out = jnp.einsum('bnhgqk,bnkhd->bnqhgd', probs.astype(v.dtype), vb)
    return out.reshape(bsz, s, Q_WIDTH)

def directional_conv(x, w, b, reverse):
    kw = w.shape[0]
    s = x.shape[1]
    if reverse:
        xp = jnp.pad(x, ((0, 0), (0, kw - 1), (0, 0)))
        y = sum(w[k] * xp[:, k:k + s] for k in range(kw))
    else:
        xp = jnp.pad(x, ((0, 0), (kw - 1, 0), (0, 0)))
        y = sum(w[k] * xp[:, kw - 1 - k:kw - 1 - k + s] for k in range(kw))
    return y + b

def centred_conv(x, w, b):
    kw = w.shape[0]
    s = x.shape[1]
    pad = (kw - 1) // 2
    xp = jnp.pad(x, ((0, 0), (pad, pad), (0, 0)))
    return sum(w[k] * xp[:, k:k + s] for k in range(kw)) + b

def rg_lru(x, w_a, b_a, w_x, b_x, lam, reverse):
    bsz, s, c = x.shape
    xb = x.reshape(bsz, s, N_RNN_BLOCKS, RNN_BLOCK_W)
    gate_a = jax.nn.sigmoid(jnp.einsum('bsnc,ncd->bsnd', xb, w_a).reshape(bsz, s, c) + b_a)
    gate_x = jax.nn.sigmoid(jnp.einsum('bsnc,ncd->bsnd', xb, w_x).reshape(bsz, s, c) + b_x)
    log_a = -RG_C * gate_a.astype(jnp.float32) * jax.nn.softplus(-lam.astype(jnp.float32))
    a = jnp.exp(log_a)
    mult = jnp.sqrt(-jnp.expm1(2.0 * log_a))
    start = jnp.arange(s) == (s - 1 if reverse else 0)
    mult = jnp.where(start[None, :, None], 1.0, mult)
    u = x.astype(jnp.float32) * gate_x.astype(jnp.float32) * mult

    def combine(left, right):
        a_l, b_l = left
        a_r, b_r = right
        return a_l * a_r, a_r * b_l + b_r

    _, h = lax.associative_scan(combine, (a, u), reverse=reverse, axis=1)
    return h.astype(x.dtype)

def setup_inputs(seed: int = 0) -> dict:
    key = jax.random.key(seed)
    ks = jax.random.split(key, 32)
    f32 = jnp.float32
    L = DEPTH

    def nrm(k, shape, scale):
        return jax.random.normal(k, shape, f32) * scale

    rad = jax.random.uniform(ks[10], (L, 2, D_RNN), f32, 0.9, 0.999)
    return {
        "x": jax.random.normal(ks[0], (BATCH, SEQ, D_MODEL), f32),
        "p": jax.random.normal(ks[1], (DEPTH, BATCH, SEQ, D_PLE), f32),
        "ln_in_g": 1.0 + nrm(ks[2], (D_MODEL,), 0.02),
        "ln_in_b": nrm(ks[3], (D_MODEL,), 0.02),
        "w_in": nrm(ks[4], (L, D_MODEL, D_IN), D_MODEL ** -0.5),
        "attn_sink": nrm(ks[5], (L, N_HEADS), 0.5),
        "rnn_conv_w": nrm(ks[6], (L, 2, RNN_CONV_W, D_RNN), RNN_CONV_W ** -0.5),
        "rnn_conv_b": nrm(ks[7], (L, 2, D_RNN), 0.02),
        "rg_w_a": nrm(ks[8], (L, 2, N_RNN_BLOCKS, RNN_BLOCK_W, RNN_BLOCK_W), RNN_BLOCK_W ** -0.5),
        "rg_b_a": nrm(ks[9], (L, 2, D_RNN), 0.02),
        "rg_w_x": nrm(ks[11], (L, 2, N_RNN_BLOCKS, RNN_BLOCK_W, RNN_BLOCK_W), RNN_BLOCK_W ** -0.5),
        "rg_b_x": nrm(ks[12], (L, 2, D_RNN), 0.02),
        "rg_lambda": jnp.log(rad) - jnp.log1p(-rad),
        "w_proj_attn": nrm(ks[13], (L, Q_WIDTH, D_MODEL), Q_WIDTH ** -0.5),
        "w_proj_rnn": nrm(ks[14], (L, D_RNN, D_MODEL), D_RNN ** -0.5),
        "w_out": nrm(ks[15], (L, D_MODEL, D_MODEL), DN_BETA * D_MODEL ** -0.5),
        "ln1_g": 1.0 + nrm(ks[16], (L, D_MODEL), 0.02),
        "ln1_b": nrm(ks[17], (L, D_MODEL), 0.02),
        "w_up": nrm(ks[18], (L, D_MODEL, 2 * D_FF), D_MODEL ** -0.5),
        "ffn_conv_w": nrm(ks[19], (L, FFN_CONV_W, D_FF), FFN_CONV_W ** -0.5),
        "ffn_conv_b": nrm(ks[20], (L, D_FF), 0.02),
        "w_down": nrm(ks[21], (L, D_FF, D_MODEL), DN_BETA * D_FF ** -0.5),
        "w_ple": nrm(ks[22], (L, D_PLE, D_MODEL), DN_BETA * D_PLE ** -0.5),
        "w_ple_gate": nrm(ks[23], (L, D_MODEL, D_MODEL), D_MODEL ** -0.5),
        "ln2_g": 1.0 + nrm(ks[24], (L, D_MODEL), 0.02),
        "ln2_b": nrm(ks[25], (L, D_MODEL), 0.02),
    }

def reference(x, p, ln_in_g, ln_in_b, w_in, attn_sink, rnn_conv_w, rnn_conv_b,
              rg_w_a, rg_b_a, rg_w_x, rg_b_x, rg_lambda, w_proj_attn, w_proj_rnn,
              w_out, ln1_g, ln1_b, w_up, ffn_conv_w, ffn_conv_b, w_down,
              w_ple, w_ple_gate, ln2_g, ln2_b):
    bsz, s, _ = x.shape
    cos, sin = rope_tables(s, x.dtype)
    split_points = np.cumsum(IN_SIZES)[:-1].tolist()
    h = layer_norm(x, ln_in_g, ln_in_b)
    for i in range(DEPTH):
        z = h @ w_in[i]
        q, k, v, xr, yr, ga, gr = jnp.split(z, split_points, axis=-1)
        q = partial_rope(q.reshape(bsz, s, N_HEADS, HEAD_DIM), cos, sin)
        k = partial_rope(k.reshape(bsz, s, N_KV_HEADS, HEAD_DIM), cos, sin)
        v = v.reshape(bsz, s, N_KV_HEADS, HEAD_DIM)
        attn = local_attention(q, k, v, attn_sink[i])

        xf = directional_conv(xr, rnn_conv_w[i, 0], rnn_conv_b[i, 0], False)
        xb = directional_conv(xr, rnn_conv_w[i, 1], rnn_conv_b[i, 1], True)
        hr = (rg_lru(xf, rg_w_a[i, 0], rg_b_a[i, 0], rg_w_x[i, 0], rg_b_x[i, 0], rg_lambda[i, 0], False)
              + rg_lru(xb, rg_w_a[i, 1], rg_b_a[i, 1], rg_w_x[i, 1], rg_b_x[i, 1], rg_lambda[i, 1], True))
        rnn = hr * jax.nn.gelu(yr)

        merged = (jax.nn.sigmoid(ga) * (attn @ w_proj_attn[i])
                  + jax.nn.sigmoid(gr) * (rnn @ w_proj_rnn[i]))
        h = layer_norm(DN_ALPHA * h + merged @ w_out[i], ln1_g[i], ln1_b[i])

        gate, val = jnp.split(h @ w_up[i], 2, axis=-1)
        gate = centred_conv(gate, ffn_conv_w[i], ffn_conv_b[i])
        ffn = (jax.nn.gelu(gate) * val) @ w_down[i]
        ple = jax.nn.sigmoid(h @ w_ple_gate[i]) * (p[i] @ w_ple[i])
        h = layer_norm(DN_ALPHA * h + ffn + ple, ln2_g[i], ln2_b[i])
    return h


_drawn_inputs = setup_inputs


def setup_inputs(seed=0):
    import zlib

    import numpy as np

    out = dict(_drawn_inputs(seed))
    spreads = {}
    factors = {'ln_in_g': 2.684,
     'attn_sink': 64.0,
     'rnn_conv_b': 5.351,
     'rg_b_a': 41.678,
     'rg_b_x': 31.023,
     'ffn_conv_b': 8.0,
     'ln_in_b': 4.951}
    for name, (base, spread) in spreads.items():
        noise = np.random.default_rng([zlib.crc32(name.encode()), seed]).standard_normal(out[name].shape)
        drawn = base * np.exp(spread * noise) if base else spread * noise
        out[name] = __import__('jax').numpy.asarray(drawn.astype(out[name].dtype))
    for name, factor in factors.items():
        out[name] = (out[name] * factor).astype(out[name].dtype)
    return out
```

```python
from contextlib import ExitStack

import numpy as np

import concourse.bass as bass
from concourse import mybir

F32 = mybir.dt.float32
F32R = mybir.dt.float32r
I32 = mybir.dt.int32
ALU = mybir.AluOpType
ACT = mybir.ActivationFunctionType
AX_X = mybir.AxisListType.X

P = 128
DEPTH, SEQ, D = 2, 256, 1024
HEADS, KV_HEADS, HEAD_DIM = 8, 2, 128
GROUP = HEADS // KV_HEADS
QK_HEADS = HEADS + KV_HEADS
ROPE_DIM = HEAD_DIM // 4
ROPE_HALF = ROPE_DIM // 2
ROPE_THETA = 500000.0
KV_WIDTH = KV_HEADS * HEAD_DIM
TT = SEQ // P
KT = D // P
RNN_BLOCKS, BLOCK_W = 4, 256
CONV_W = 4
D_FF = 3 * D
FF_TILES = D_FF // P
FF_GROUPS = D_FF // 512
D_PLE = 256
LN_EPS = 1e-5
ALPHA = float((2 * DEPTH) ** 0.25)
SCALE = float(HEAD_DIM) ** -0.5
MASKED = -1e30
RSQRT_MAGIC = 1597463007.0

Q0 = 0
K0 = HEADS * HEAD_DIM
XR0 = K0 + 2 * KV_WIDTH
YR0 = XR0 + D
GA0 = YR0 + D
GR0 = GA0 + D

UNITS = [
    ("q0", "token", "w_in", Q0), ("q1", "token", "w_in", Q0 + 512), ("kv", "token", "w_in", K0),
    ("xr0", "feature", "w_in", XR0), ("xr1", "feature", "w_in", XR0 + 512),
    ("yr0", "feature", "w_in", YR0), ("yr1", "feature", "w_in", YR0 + 512),
    ("rg0", "gates", None, 0), ("rg1", "gates", None, 1),
    ("ga0", "token", "w_in", GA0), ("ga1", "token", "w_in", GA0 + 512),
    ("gr0", "token", "w_in", GR0), ("gr1", "token", "w_in", GR0 + 512),
    ("pa0", "token", "w_proj_attn", 0), ("pa1", "token", "w_proj_attn", 512),
    ("pr0", "token", "w_proj_rnn", 0), ("pr1", "token", "w_proj_rnn", 512),
    ("wo0", "token", "w_out", 0), ("wo1", "token", "w_out", 512),
    ("ple", "ple", "w_ple", 0),
]
for _j in range(FF_GROUPS):
    UNITS += [(f"g{_j}", "feature", "w_up", 512 * _j), (f"v{_j}", "feature", "w_up", D_FF + 512 * _j)]
    if _j:
        UNITS += [(f"d{_j - 1}", "down", "w_down", _j - 1)]
UNITS += [("pg0", "token", "w_ple_gate", 0), ("pg1", "token", "w_ple_gate", 512),
          (f"d{FF_GROUPS - 1}", "down", "w_down", FF_GROUPS - 1)]
KIND = {name: kind for name, kind, _, _ in UNITS}
HALVES = [(u, hh) for u in UNITS for hh in range(2)]
FIRST_HALF = {u[0]: 2 * n for n, u in enumerate(UNITS)}
W_SLOTS = 3
RAW_SLOTS = 3
AHEAD = 2


def half_size(n):
    return 1024 if HALVES[n][0][1] == "ple" else 2048


def half_loads(n):
    return 2 if HALVES[n][0][1] == "gates" else 1


LOADED = []
_at = [0] * RAW_SLOTS
for _n in range(len(HALVES)):
    _at[_n % RAW_SLOTS] += 16 * half_loads(_n)
    LOADED.append(_at[_n % RAW_SLOTS])
LOADED_PER_LAYER = list(_at)

PRODUCT = {}
AFTER_HALF = []
_c = 0
for (_name, _kind, _, _), _hh in HALVES:
    if _kind == "token":
        _parts = [("half",)] if _hh == 0 else [0, 1]
    elif _kind == "feature":
        _parts = [_hh]
    elif _kind == "gates":
        _parts = [(b, g) for b in (2 * _hh, 2 * _hh + 1) for g in range(2)]
    elif _kind == "ple":
        _parts = [(_hh, t) for t in range(TT)]
    else:
        _parts = [("half",)] if _hh == 0 else [0, 1]
    for _p in _parts:
        _c += 1
        PRODUCT[_name, _p] = _c
    AFTER_HALF.append(_c)

RING = {}
_uses = [0] * 4
_pair = 0
for _name, _kind, _, _ in UNITS:
    if _kind in ("token", "feature"):
        _sets = [[(_name, 0), (_name, 1)]]
    elif _kind == "gates":
        _sets = [[(_name, (b, 0)), (_name, (b, 1))] for b in range(RNN_BLOCKS)]
    elif _kind == "ple":
        _sets = [[(_name, (n, 0)), (_name, (n, 1))] for n in range(2)]
    else:
        _sets = []
    for _set in _sets:
        for _b, _key in enumerate(_set):
            _bank = 2 * (_pair % 2) + _b
            RING[_key] = (_bank, _uses[_bank])
            _uses[_bank] += 1
        _pair += 1
RING_USES = list(_uses)

GROUPS = 2 * RNN_BLOCKS // 2
ROUNDS = KV_HEADS * TT
LN_STEPS = 13
PER = dict(
    split=len(HALVES), hi_part=len(HALVES), products=AFTER_HALF[-1],
    ln_step=2 * TT * LN_STEPS, ln_norm=2 * TT, x_turned=3 * 4, x_hi=3 * 4, x_ready=3 * 4,
    rope_step=6, qk_turned=5, qk_ready=5,
    scores=ROUNDS, soft_step=6 * ROUNDS, exp_done=5 * ROUNDS, probs=ROUNDS, probs_turned=ROUNDS,
    probs_back=ROUNDS, mixed=ROUNDS, attn_hi=ROUNDS, attn_ready=ROUNDS,
    param_step=16, param_exp=1, conv_base=8, conv_step=48, rin_hi=8, rin_ready=8,
    decay=16, pair_ready=8, m2_done=8, gated=8, root=GROUPS, rg_step=3 * GROUPS, scanned=GROUPS,
    rnn_step=4, rnn_hi=2, rnn_ready=2, merge=4, p_turned=1, p_hi=1, p_ready=1,
    gate_base=12, tap_step=24, gelu=12, f_hi=12, f_ready=12, tail_step=4,
)


HEAD_START = ["products", "p_turned", "split", "ln_norm", "rnn_ready", "f_ready", "gated", "m2_done", "scanned",
              "tail_step"]
BASE = {name: 1 for name in HEAD_START}


def hybrid_encoder(nc, a, out):
    with ExitStack() as ctx:
        def sb(name, shape, dt=F32):
            return ctx.enter_context(nc.sbuf_tensor("sb_" + name, shape, dt))

        def sem(name):
            return ctx.enter_context(nc.semaphore(name))

        w_hi = sb("w_hi", [P, W_SLOTS, 2048], F32R)
        w_lo = sb("w_lo", [P, W_SLOTS, 2048], F32R)
        x_hi = sb("x_hi", [P, KT, SEQ], F32R)
        x_lo = sb("x_lo", [P, KT, SEQ], F32R)
        a_hi = sb("a_hi", [P, KT, SEQ], F32R)
        a_lo = sb("a_lo", [P, KT, SEQ], F32R)
        r_hi = sb("r_hi", [P, KT, SEQ], F32R)
        r_lo = sb("r_lo", [P, KT, SEQ], F32R)

        raw = sb("raw", [P, RAW_SLOTS, 2048])
        h = sb("h", [P, TT, D])
        lnp = sb("lnp", [P, 2, D])
        qk = sb("qk", [P, TT, QK_HEADS, HEAD_DIM])
        v = sb("v", [P, TT, KV_HEADS, HEAD_DIM])
        qkT = sb("qkT", [P, QK_HEADS, SEQ])
        yg = qk[:, :, :, :].rearrange("p t h d -> p (t h d)")[:, 0:KT * SEQ].rearrange(
            "p (k s) -> p k s", k=KT)
        hf = qkT[:, 0:KT, :]
        hb = sb("hb", [P, KT, SEQ])
        xT = sb("xT", [P, KT, SEQ])
        ga = sb("ga", [P, TT, D])
        gr = xT[:, :, :].rearrange("p (t a) s -> p t (a s)", t=TT)
        soft = sb("soft", [P, GROUP, SEQ])
        pT = sb("pT", [P, TT, GROUP, P])
        decay_a = soft
        root_m = pT[:, :, :, :].rearrange("p a g t -> p (a g t)").rearrange("p (k s) -> p k s", k=4)
        tmp = sb("tmp", [P, 6, 2, SEQ])
        xc, ta, tx = tmp[:, 0:2], tmp[:, 2:4], tmp[:, 4:6]
        p_in = sb("p_in", [P, TT, D_PLE])
        rnnp = sb("rnnp", [P, 2, KT, 8])
        rnnd = sb("rnnd", [P, 2, 2, KT])
        coef = sb("coef", [P, 2, 2, KT])
        lam_t = sb("lam_t", [P, 6, 2, KT])
        ffnp = sb("ffnp", [P, FF_TILES, 4])
        sink = sb("sink", [P, HEADS])
        nsink = sb("nsink", [P, HEADS])
        rope = sb("rope", [P, 2, TT, ROPE_HALF])
        rope_size = TT * QK_HEADS * ROPE_HALF
        rope_t = tmp[:, 2:6].rearrange("p a b s -> p (a b s)")[:, 0:4 * rope_size].rearrange(
            "p (i t h c) -> p i t h c", i=4, t=TT, h=QK_HEADS)
        masks = sb("masks", [P, 2, P])
        ident = sb("ident", [P, P])
        st = sb("st", [P, TT, 2, 6])
        mv = sb("mv", [P, TT, 8])
        sm = sb("sm", [P, 6, GROUP])

        ring = ctx.enter_context(nc.psum_tensor("ring", [P, 4, 512], F32))
        misc = ctx.enter_context(nc.psum_tensor("misc", [P, 4, 512], F32))

        s_raw = [sem(f"raw_loaded{i}") for i in range(RAW_SLOTS)]
        s_emptied = [sem(f"bank_emptied{i}") for i in range(4)]
        s_split = sem("split")
        s_hi_part = sem("hi_part")
        s_products = sem("products")
        s_ln_step = sem("ln_step")
        s_ln_norm = sem("ln_norm")
        s_x_turned = sem("x_turned")
        s_x_hi = sem("x_hi")
        s_x_ready = sem("x_ready")
        s_rope_step = sem("rope_step")
        s_qk_turned = sem("qk_turned")
        s_qk_ready = sem("qk_ready")
        s_scores = sem("scores")
        s_soft_step = sem("soft_step")
        s_exp_done = sem("exp_done")
        s_probs = sem("probs")
        s_probs_turned = sem("probs_turned")
        s_probs_back = sem("probs_back")
        s_mixed = sem("mixed")
        s_attn_hi = sem("attn_hi")
        s_attn_ready = sem("attn_ready")
        s_param_step = sem("param_step")
        s_param_exp = sem("param_exp")
        s_conv_base = sem("conv_base")
        s_conv_step = sem("conv_step")
        s_rin_hi = sem("rin_hi")
        s_rin_ready = sem("rin_ready")
        s_decay = sem("decay")
        s_pair_ready = sem("pair_ready")
        s_m2_done = sem("m2_done")
        s_gated = sem("gated")
        s_root = sem("root")
        s_rg_step = sem("rg_step")
        s_scanned = sem("scanned")
        s_rnn_step = sem("rnn_step")
        s_rnn_hi = sem("rnn_hi")
        s_rnn_ready = sem("rnn_ready")
        s_merge = sem("merge")
        s_p_turned = sem("p_turned")
        s_p_hi = sem("p_hi")
        s_p_ready = sem("p_ready")
        s_gate_base = sem("gate_base")
        s_tap_step = sem("tap_step")
        s_gelu = sem("gelu")
        s_f_hi = sem("f_hi")
        s_f_ready = sem("f_ready")
        s_tail_step = sem("tail_step")
        s_h = sem("h_loaded")
        s_lnp = sem("lnp_loaded")
        s_small = sem("rnn_params_loaded")
        s_ffnp = sem("ffn_params_loaded")
        s_p = sem("p_loaded")
        s_const = sem("constants")
        s_rope = sem("rope_loaded")
        s_out = sem("out_stored")

        def value(name, l, count):
            return l * PER[name] + count + BASE.get(name, 0)

        def made(l, name, part):
            return value("products", l, PRODUCT[name, part])

        def read_out(l, key):
            return l * RING_USES[RING[key][0]] + RING[key][1] + 2

        def free(l, key):
            return read_out(l, key) - 1

        def all_emptied(eng, l, keys):
            latest = {}
            for key in keys:
                bank, before = RING[key]
                latest[bank] = max(latest.get(bank, 0), before + 1)
            for bank, count in latest.items():
                eng.wait_ge(s_emptied[bank], l * RING_USES[bank] + count + 1)

        def bank_of(key):
            return ring[:, RING[key][0], :]

        block = ctx.enter_context(nc.Block())

        @block.sync
        def _(sp):
            def half_source(l, n):
                (name, kind, src, first), hh = HALVES[n]
                if kind == "gates":
                    return [a[w][bass.ds(l, 1), first, 2 * hh:2 * hh + 2].rearrange(
                        "a b (k p) d -> p (a b k) d", p=P) for w in ("rg_w_a", "rg_w_x")]
                view = a[src][bass.ds(l, 1)].rearrange("a (k p) n -> p (a k) n", p=P)
                if kind == "token":
                    return [view[:, 4 * hh:4 * hh + 4, first:first + 512]]
                if kind == "feature":
                    return [view[:, :, first + 256 * hh:first + 256 * hh + 256]]
                if kind == "ple":
                    return [view[:, :, 512 * hh:512 * hh + 512]]
                return [view[:, 4 * first + 2 * hh:4 * first + 2 * hh + 2, :]]

            def load_half(l, n):
                sp.wait_ge(s_split, value("split", l, max(0, n - RAW_SLOTS + 1)))
                slot = n % RAW_SLOTS
                parts = half_source(l, n)
                step = half_size(n) // len(parts)
                for i, src in enumerate(parts):
                    dst = raw[:, slot, i * step:(i + 1) * step].rearrange("p (k n) -> p k n", k=src.shape[1])
                    sp.dma_start(dst, src).then_inc(s_raw[slot], 16)

            sp.dma_start(h[:, 0, :], a["x"][0, 0:P, :]).then_inc(s_h, 16)
            sp.dma_start(h[:, 1, :], a["x"][0, P:SEQ, :]).then_inc(s_h, 16)
            sp.dma_start(rope[:], a["rope"]).then_inc(s_rope, 16)
            with sp.Fori(0, DEPTH) as l:
                sp.wait_ge(s_ln_norm, value("ln_norm", l, 0))
                sp.dma_start(lnp[:], a["ln"][bass.ds(2 * l, 1)].to_broadcast((P, 2, D))).then_inc(s_lnp, 16)
                load_half(l, 0)
                load_half(l, 1)
                sp.wait_ge(s_rnn_ready, value("rnn_ready", l, 0))
                sp.dma_start(rnnp[:], a["rnnp"][bass.ds(l, 1)].rearrange("a p d k c -> p (a d) k c")
                             ).then_inc(s_small, 16)
                sp.dma_start(sink[:], a["attn_sink"][bass.ds(l, 1)].to_broadcast((P, HEADS))).then_inc(s_small, 16)
                sp.wait_ge(s_p_turned, value("p_turned", l, 0))
                sp.dma_start(p_in[:], a["p"][bass.ds(l, 1), 0].rearrange("a (t q) c -> q (a t) c", q=P)
                             ).then_inc(s_p, 16)
                for n in range(2, FIRST_HALF["pa0"]):
                    load_half(l, n)
                sp.wait_ge(s_ln_norm, value("ln_norm", l, TT))
                sp.dma_start(lnp[:], a["ln"][bass.ds(2 * l + 1, 1)].to_broadcast((P, 2, D))).then_inc(s_lnp, 16)
                sp.wait_ge(s_f_ready, value("f_ready", l, 0))
                sp.dma_start(ffnp[:], a["ffnp"][bass.ds(l, 1)].rearrange("a p k c -> p (a k) c")
                             ).then_inc(s_ffnp, 16)
                for n in range(FIRST_HALF["pa0"], len(HALVES)):
                    load_half(l, n)
            sp.wait_ge(s_ln_norm, value("ln_norm", DEPTH, 0))
            sp.dma_start(lnp[:], a["ln"][2 * DEPTH:2 * DEPTH + 1].to_broadcast((P, 2, D))).then_inc(s_lnp, 16)
            for t in range(TT):
                sp.wait_ge(s_ln_norm, value("ln_norm", DEPTH, t + 1))
                sp.dma_start(out[0, t * P:(t + 1) * P, :], h[:, t, :]).then_inc(s_out, 16)
            sp.wait_ge(s_out, 16 * TT)

        @block.gpsimd
        def _(pool):
            nc.gpsimd.memset(ident[:], 0.0).then_inc(s_const, 1)
            nc.gpsimd.memset(masks[:], 0.0).then_inc(s_const, 1)
            pool.wait_ge(s_const, 2)
            nc.gpsimd.affine_select(out=ident[:], in_=ident[:], compare_op=ALU.not_equal, fill=1.0, base=0,
                                    pattern=[[-1, P]], channel_multiplier=1).then_inc(s_const, 1)
            nc.gpsimd.affine_select(out=masks[:, 0, :], in_=masks[:, 0, :], compare_op=ALU.is_ge, fill=MASKED,
                                    base=0, pattern=[[-1, P]], channel_multiplier=1).then_inc(s_const, 1)
            nc.gpsimd.affine_select(out=masks[:, 1, :], in_=masks[:, 1, :], compare_op=ALU.is_ge, fill=MASKED,
                                    base=0, pattern=[[1, P]], channel_multiplier=-1).then_inc(s_const, 1)

        @block.tensor
        def _(pe):
            def three(dst, lhs, rhs, first, last):
                nc.tensor.matmul(dst, lhs[0], rhs[0], start=first, stop=False)
                nc.tensor.matmul(dst, lhs[0], rhs[1], start=False, stop=False)
                return nc.tensor.matmul(dst, lhs[1], rhs[0], start=False, stop=last)

            def weights(l, n):
                pe.wait_ge(s_split, value("split", l, n + 1))
                return n % W_SLOTS

            def token_half(l, n, left):
                name, hh = HALVES[n][0][0], HALVES[n][1]
                slot = weights(l, n)
                for t in range(TT):
                    if hh == 0:
                        pe.wait_ge(s_emptied[RING[(name, t)][0]], free(l, (name, t)))
                    for k in range(4):
                        kk = 4 * hh + k
                        cols = slice(512 * k, 512 * k + 512)
                        last = three(bank_of((name, t)), [x[:, kk, t * P:(t + 1) * P] for x in left],
                                     [w_hi[:, slot, cols], w_lo[:, slot, cols]], kk == 0, kk == KT - 1)
                    if hh == 1 or t == TT - 1:
                        last.then_inc(s_products, 1)

            def feature_tile(l, n, j):
                name, hh = HALVES[n][0][0], HALVES[n][1]
                slot = weights(l, n)
                if j == 0:
                    pe.wait_ge(s_emptied[RING[(name, hh)][0]], free(l, (name, hh)))
                dst = bank_of((name, hh))[:, SEQ * j:SEQ * (j + 1)]
                for k in range(KT):
                    cols = slice(256 * k + P * j, 256 * k + P * (j + 1))
                    last = three(dst, [w_hi[:, slot, cols], w_lo[:, slot, cols]],
                                 [x_hi[:, k, :], x_lo[:, k, :]], k == 0, k == KT - 1)
                if j == 1:
                    last.then_inc(s_products, 1)

            def feature_unit(l, name):
                for n in (FIRST_HALF[name], FIRST_HALF[name] + 1):
                    for j in range(2):
                        feature_tile(l, n, j)

            def token_unit(l, name, left):
                for n in (FIRST_HALF[name], FIRST_HALF[name] + 1):
                    token_half(l, n, left)

            def gates_unit(l, direction):
                for hh in range(2):
                    n = FIRST_HALF[f"rg{direction}"] + hh
                    slot = weights(l, n)
                    for b in (2 * hh, 2 * hh + 1):
                        pe.wait_ge(s_rin_ready, value("rin_ready", l, 4 * direction + b + 1))
                        for g in range(2):
                            key = (f"rg{direction}", (b, g))
                            pe.wait_ge(s_emptied[RING[key][0]], free(l, key))
                            for d in range(2):
                                for k in range(2):
                                    at = 1024 * g + 256 * (2 * (b % 2) + k) + P * d
                                    last = three(bank_of(key)[:, SEQ * d:SEQ * (d + 1)],
                                                 [w_hi[:, slot, at:at + P], w_lo[:, slot, at:at + P]],
                                                 [r_hi[:, 2 * b + k, :], r_lo[:, 2 * b + k, :]], k == 0, k == 1)
                            last.then_inc(s_products, 1)

            def ple_unit(l):
                pe.wait_ge(s_p_ready, value("p_ready", l, 1))
                for hh in range(2):
                    slot = weights(l, FIRST_HALF["ple"] + hh)
                    for t in range(TT):
                        key = ("ple", (hh, t))
                        pe.wait_ge(s_emptied[RING[key][0]], free(l, key))
                        for k in range(2):
                            cols = slice(512 * k, 512 * k + 512)
                            last = three(bank_of(key), [r_hi[:, k, t * P:(t + 1) * P], r_lo[:, k, t * P:(t + 1) * P]],
                                         [w_hi[:, slot, cols], w_lo[:, slot, cols]], k == 0, k == 1)
                        last.then_inc(s_products, 1)

            def down_unit(l, j):
                for hh in range(2):
                    slot = weights(l, FIRST_HALF[f"d{j}"] + hh)
                    pe.wait_ge(s_f_ready, value("f_ready", l, 2 * j + hh + 1))
                    for t in range(TT):
                        for c in range(2):
                            for k in range(2):
                                cols = slice(1024 * k + 512 * c, 1024 * k + 512 * (c + 1))
                                kk = 4 * (j % 2) + 2 * hh + k
                                last = three(misc[:, 2 * t + c, :],
                                             [a_hi[:, kk, t * P:(t + 1) * P], a_lo[:, kk, t * P:(t + 1) * P]],
                                             [w_hi[:, slot, cols], w_lo[:, slot, cols]],
                                             j == 0 and hh == 0 and k == 0,
                                             j == FF_GROUPS - 1 and hh == 1 and k == 1)
                        if hh == 1 or t == TT - 1:
                            last.then_inc(s_products, 1)

            def turn(dst, src):
                return nc.tensor.transpose(dst, src, ident[:])

            def turn_rows(src, t, c):
                for k in range(4):
                    last = turn(misc[:, 2 * t + c, k * P:(k + 1) * P], src[:, t, (4 * c + k) * P:(4 * c + k + 1) * P])
                last.then_inc(s_x_turned, 1)

            def turn_h(l, norm):
                for t in range(TT):
                    pe.wait_ge(s_ln_norm, value("ln_norm", l, TT * norm + t + 1))
                    for c in range(2):
                        turn_rows(h, t, c)

            def x_ready(l, kind):
                pe.wait_ge(s_x_ready, value("x_ready", l, 4 * (kind + 1)))

            def turn_qk(l):
                pe.wait_ge(s_rope_step, value("rope_step", l, 6))
                for i in range(QK_HEADS // 2):
                    if i == 4:
                        pe.wait_ge(s_qk_ready, value("qk_ready", l, 1))
                    for j in range(2):
                        for t in range(TT):
                            last = turn(misc[:, i % 4, (2 * j + t) * P:(2 * j + t + 1) * P], qk[:, t, 2 * i + j, :])
                    last.then_inc(s_qk_turned, 1)

            def scores(l, r):
                g, b = divmod(r, TT)
                if r == 0:
                    pe.wait_ge(s_qk_ready, value("qk_ready", l, 5))
                else:
                    pe.wait_ge(s_exp_done, value("exp_done", l, 5 * r))
                for i in range(GROUP):
                    last = nc.tensor.matmul(misc[:, i // 2, SEQ * (i % 2):SEQ * (i % 2 + 1)],
                                            qkT[:, GROUP * g + i, b * P:(b + 1) * P], qkT[:, HEADS + g, :],
                                            start=True, stop=True)
                last.then_inc(s_scores, 1)

            def turn_probs(l, r):
                pe.wait_ge(s_probs, value("probs", l, r + 1))
                if r:
                    pe.wait_ge(s_attn_ready, value("attn_ready", l, r))
                for kb in range(TT):
                    for i in range(GROUP):
                        last = turn(misc[:, 2 + kb, i * P:(i + 1) * P], soft[:, i, kb * P:(kb + 1) * P])
                last.then_inc(s_probs_turned, 1)

            def mix_values(l, r):
                pe.wait_ge(s_probs_back, value("probs_back", l, r + 1))
                for kb in range(TT):
                    last = nc.tensor.matmul(misc[:, 2, :], v[:, kb, r // TT, :], pT[:, kb, :, :],
                                            start=kb == 0, stop=kb == TT - 1)
                last.then_inc(s_mixed, 1)

            for begin in (s_products, s_p_turned):
                pe.sem_inc(begin, 1)
            pe.wait_ge(s_const, 5)
            with pe.Fori(0, DEPTH) as l:
                x = (x_hi, x_lo)
                turn_h(l, 0)
                x_ready(l, 0)
                token_unit(l, "q0", x)
                token_unit(l, "q1", x)
                token_unit(l, "kv", x)
                feature_unit(l, "xr0")
                turn_qk(l)
                n = FIRST_HALF["xr1"]
                feature_tile(l, n, 0)
                feature_tile(l, n, 1)
                scores(l, 0)
                feature_tile(l, n + 1, 0)
                feature_tile(l, n + 1, 1)
                turn_probs(l, 0)
                scores(l, 1)
                feature_tile(l, n + 2, 0)
                mix_values(l, 0)
                feature_tile(l, n + 2, 1)
                turn_probs(l, 1)
                scores(l, 2)
                feature_tile(l, n + 3, 0)
                mix_values(l, 1)
                feature_tile(l, n + 3, 1)
                turn_probs(l, 2)
                scores(l, 3)
                feature_tile(l, n + 4, 0)
                mix_values(l, 2)
                feature_tile(l, n + 4, 1)
                turn_probs(l, 3)
                feature_tile(l, n + 5, 0)
                mix_values(l, 3)
                feature_tile(l, n + 5, 1)
                gates_unit(l, 0)
                gates_unit(l, 1)
                for name in ("ga0", "ga1", "gr0", "gr1"):
                    token_unit(l, name, x)
                pe.wait_ge(s_attn_ready, value("attn_ready", l, ROUNDS))
                token_unit(l, "pa0", (a_hi, a_lo))
                token_unit(l, "pa1", (a_hi, a_lo))
                pe.wait_ge(s_rnn_ready, value("rnn_ready", l, 2))
                token_unit(l, "pr0", (r_hi, r_lo))
                token_unit(l, "pr1", (r_hi, r_lo))
                pe.wait_ge(s_p, 16 * l + 16)
                for k in range(2):
                    for t in range(TT):
                        last = turn(misc[:, 0, (2 * k + t) * P:(2 * k + t + 1) * P], p_in[:, t, k * P:(k + 1) * P])
                last.then_inc(s_p_turned, 1)
                pe.wait_ge(s_p_ready, value("p_ready", l, 1))
                for c in range(2):
                    for t in range(TT):
                        pe.wait_ge(s_merge, value("merge", l, 2 * c + t + 1))
                        turn_rows(ga, t, c)
                x_ready(l, 1)
                token_unit(l, "wo0", x)
                token_unit(l, "wo1", x)
                ple_unit(l)
                turn_h(l, 1)
                x_ready(l, 2)
                for j in range(FF_GROUPS):
                    feature_unit(l, f"g{j}")
                    feature_unit(l, f"v{j}")
                    if j:
                        down_unit(l, j - 1)
                token_unit(l, "pg0", x)
                token_unit(l, "pg1", x)
                down_unit(l, FF_GROUPS - 1)

        @block.scalar
        def _(act):
            def split_hi(l, n):
                slot = n % RAW_SLOTS
                act.wait_ge(s_raw[slot], l * LOADED_PER_LAYER[slot] + LOADED[n])
                act.wait_ge(s_products, value("products", l, AFTER_HALF[n - W_SLOTS] if n >= W_SLOTS else 0))
                size = half_size(n)
                nc.scalar.copy(w_hi[:, n % W_SLOTS, 0:size], raw[:, slot, 0:size]).then_inc(s_hi_part, 1)

            split = [0]

            def split_to(l, n):
                while split[0] <= min(n, len(HALVES) - 1):
                    split_hi(l, split[0])
                    split[0] += 1

            def x_parts(l, kind, order, scale):
                for i, (t, c) in enumerate(order):
                    act.wait_ge(s_x_turned, value("x_turned", l, 4 * kind + i + 1))
                    nc.scalar.activation(x_hi[:, 4 * c:4 * c + 4, t * P:(t + 1) * P], misc[:, 2 * t + c, :].rearrange("p (k t) -> p k t", k=4), ACT.Copy,
                                         scale=scale).then_inc(s_x_hi, 1)

            def out_of(l, name, part, dst, func, scale=1.0):
                key = (name, part)
                act.wait_ge(s_products, made(l, name, part))
                nc.scalar.activation(dst, bank_of(key), func, scale=scale).then_inc(s_emptied[RING[key][0]], 1)

            def conv_base(l, i):
                direction, b = divmod(i, RNN_BLOCKS)
                if i == 0:
                    act.wait_ge(s_small, 32 * l + 32)
                if b % 2 == 0:
                    all_emptied(act, l, [(f"xr{b // 2}", hh) for hh in range(2)])
                act.wait_ge(s_gated, value("gated", l, max(0, i - 1)))
                for j in range(2):
                    ft = 2 * b + j
                    last = nc.scalar.activation(xc[:, i % 2, j, :], xT[:, ft, :], ACT.Identity,
                                                bias=rnnp[:, direction, ft, 4:5], scale=rnnp[:, direction, ft, 0:1])
                last.then_inc(s_conv_base, 1)

            def conv_hi(l, i):
                direction, b = divmod(i, RNN_BLOCKS)
                act.wait_ge(s_conv_step, value("conv_step", l, 6 * (i + 1)))
                if direction:
                    act.wait_ge(s_products, made(l, "rg0", (b, 1)))
                nc.scalar.activation(r_hi[:, 2 * b:2 * b + 2, :], xc[:, i % 2], ACT.Copy,
                                     scale=1.0).then_inc(s_rin_hi, 1)

            def gate_curves(l, i):
                direction, b = divmod(i, RNN_BLOCKS)
                name = f"rg{direction}"
                if i == 0:
                    act.wait_ge(s_param_step, value("param_step", l, PER["param_step"]))
                act.wait_ge(s_m2_done, value("m2_done", l, max(0, i - 1)))
                act.wait_ge(s_gated, value("gated", l, max(0, i - 1)))
                for g, dst in ((0, ta), (1, tx)):
                    key = (name, (b, g))
                    act.wait_ge(s_products, made(l, name, (b, g)))
                    for d in range(2):
                        last = nc.scalar.activation(dst[:, i % 2, d, :], bank_of(key)[:, SEQ * d:SEQ * (d + 1)],
                                                    ACT.Tanh, bias=rnnd[:, g, direction, 2 * b + d:2 * b + d + 1],
                                                    scale=0.5)
                    last.then_inc(s_emptied[RING[key][0]], 1)
                if b % 2 == 0:
                    act.wait_ge(s_scanned, value("scanned", l, i // 2))
                act.wait_ge(s_emptied[RING[(name, (b, 0))][0]], read_out(l, (name, (b, 0))))
                at = 2 * (b % 2)
                for d in range(2):
                    ft = 2 * b + d
                    last = nc.scalar.activation(decay_a[:, at + d, :], ta[:, i % 2, d, :], ACT.Exp,
                                                bias=coef[:, 1, direction, ft:ft + 1],
                                                scale=coef[:, 1, direction, ft:ft + 1])
                last.then_inc(s_decay, 1)
                for d in range(2):
                    ft = 2 * b + d
                    last = nc.scalar.activation(root_m[:, at + d, :], ta[:, i % 2, d, :], ACT.Tanh,
                                                bias=coef[:, 0, direction, ft:ft + 1],
                                                scale=coef[:, 0, direction, ft:ft + 1])
                last.then_inc(s_decay, 1)
                act.wait_ge(s_decay, value("decay", l, 2 * i + 2))
                nc.scalar.activation(ta[:, i % 2], decay_a[:, at:at + 2, :], ACT.Square).then_inc(s_pair_ready, 1)

            def root(l, g):
                act.wait_ge(s_m2_done, value("m2_done", l, 2 * g + 2))
                nc.scalar.activation(root_m, root_m, ACT.Sqrt, scale=0.25).then_inc(s_root, 1)

            def rnn_out(l, c):
                act.wait_ge(s_rnn_step, value("rnn_step", l, 2 * c + 2))
                nc.scalar.activation(r_hi[:, 4 * c:4 * c + 4, :], hf[:, 4 * c:4 * c + 4, :], ACT.Copy,
                                     scale=1.0).then_inc(s_rnn_hi, 1)

            def exponentials(l, r):
                act.wait_ge(s_soft_step, value("soft_step", l, 6 * r + 4))
                for i in range(GROUP):
                    nc.scalar.activation(soft[:, i, :], misc[:, i // 2, SEQ * (i % 2):SEQ * (i % 2 + 1)], ACT.Exp,
                                         bias=sm[:, 1, i:i + 1], scale=SCALE,
                                         accum_out=sm[:, 3, i:i + 1]).then_inc(s_exp_done, 1)
                nc.scalar.activation(sm[:, 4, :], sm[:, 2, :], ACT.Exp).then_inc(s_exp_done, 1)

            def probs_back(l, r):
                act.wait_ge(s_probs_turned, value("probs_turned", l, r + 1))
                nc.scalar.copy(pT[:, :, :, :].rearrange("p a g t -> p (a g t)"),
                               misc[:, 2:4, :].rearrange("p a n -> p (a n)")).then_inc(s_probs_back, 1)

            def attn_out(l, r):
                g, b = divmod(r, TT)
                act.wait_ge(s_mixed, value("mixed", l, r + 1))
                nc.scalar.activation(a_hi[:, GROUP * g:GROUP * (g + 1), b * P:(b + 1) * P], misc[:, 2, :].rearrange("p (i t) -> p i t", i=GROUP), ACT.Copy,
                                     scale=1.0).then_inc(s_attn_hi, 1)

            def gate_base(l, j, hh):
                if j == 0 and hh == 0:
                    act.wait_ge(s_ffnp, 16 * l + 16)
                act.wait_ge(s_products, made(l, f"g{j}", hh))
                act.wait_ge(s_f_ready, value("f_ready", l, max(0, 2 * (j - 2) + hh + 1)))
                for d in range(2):
                    ft = 4 * j + 2 * hh + d
                    last = nc.scalar.activation(tmp[:, hh + 2 * (j % 2), d, :],
                                                bank_of((f"g{j}", hh))[:, SEQ * d:SEQ * (d + 1)], ACT.Identity,
                                                bias=ffnp[:, ft, 3:4], scale=ffnp[:, ft, 1:2])
                last.then_inc(s_gate_base, 1)

            def gelu(l, j, hh):
                act.wait_ge(s_emptied[RING[(f"g{j}", hh)][0]], read_out(l, (f"g{j}", hh)))
                c = tmp[:, hh + 2 * (j % 2)]
                nc.scalar.activation(c, c, ACT.Gelu_apprx_tanh).then_inc(s_gelu, 1)

            def hidden_hi(l, j, hh):
                act.wait_ge(s_emptied[RING[(f"v{j}", hh)][0]], read_out(l, (f"v{j}", hh)))
                if j >= 2 and hh == 0:
                    act.wait_ge(s_products, value("products", l, PRODUCT[f"d{j - 2}", 1]))
                at = 4 * (j % 2) + 2 * hh
                nc.scalar.activation(a_hi[:, at:at + 2, :], tmp[:, hh + 2 * (j % 2)], ACT.Copy,
                                     scale=1.0).then_inc(s_f_hi, 1)

            with act.Fori(0, DEPTH) as l:
                split[0] = 0
                split_to(l, 2)
                x_parts(l, 0, [(t, c) for t in range(TT) for c in range(2)], 1.0)
                act.wait_ge(s_param_step, value("param_step", l, 1))
                nc.scalar.activation(lam_t[:, 1], lam_t[:, 0], ACT.Exp).then_inc(s_param_exp, 1)
                for i, name in enumerate(("q0", "q1")):
                    split_to(l, FIRST_HALF[name] + 1 + AHEAD)
                    for t in range(TT):
                        out_of(l, name, t, qk[:, t, 4 * i:4 * i + 4, :].rearrange("p h d -> p (h d)"), ACT.Copy)
                split_to(l, FIRST_HALF["kv"] + 1 + AHEAD)
                for t in range(TT):
                    act.wait_ge(s_products, made(l, "kv", t))
                    nc.scalar.copy(qk[:, t, HEADS:QK_HEADS, :].rearrange("p h d -> p (h d)"),
                                   bank_of(("kv", t))[:, 0:KV_WIDTH])
                    nc.scalar.copy(v[:, t].rearrange("p h d -> p (h d)"),
                                   bank_of(("kv", t))[:, KV_WIDTH:2 * KV_WIDTH]).then_inc(
                        s_emptied[RING["kv", t][0]], 1)
                for hh in range(2):
                    split_to(l, FIRST_HALF["xr0"] + hh + AHEAD)
                    out_of(l, "xr0", hh, xT[:, 2 * hh:2 * hh + 2, :].rearrange("p k s -> p (k s)"), ACT.Copy)
                conv_base(l, 0)
                for i in range(5):
                    act.wait_ge(s_qk_turned, value("qk_turned", l, i + 1))
                    nc.scalar.copy(qkT[:, 2 * i:2 * i + 2, :].rearrange("p k s -> p (k s)"),
                                   misc[:, i % 4, :]).then_inc(s_qk_ready, 1)
                split_to(l, FIRST_HALF["xr1"] + AHEAD)
                out_of(l, "xr1", 0, xT[:, 4:6, :].rearrange("p k s -> p (k s)"), ACT.Copy)
                conv_hi(l, 0)
                conv_base(l, 1)
                exponentials(l, 0)
                split_to(l, FIRST_HALF["xr1"] + 1 + AHEAD)
                out_of(l, "xr1", 1, xT[:, 6:8, :].rearrange("p k s -> p (k s)"), ACT.Copy)
                conv_hi(l, 1)
                exponentials_of = {0: 1, 1: 2, 2: 3}
                probs_back(l, 0)
                exponentials(l, exponentials_of[0])
                split_to(l, FIRST_HALF["yr0"] + AHEAD)
                attn_out(l, 0)
                out_of(l, "yr0", 0, yg[:, 0:2, :].rearrange("p k s -> p (k s)"), ACT.Gelu_apprx_tanh)
                probs_back(l, 1)
                exponentials(l, exponentials_of[1])
                split_to(l, FIRST_HALF["yr0"] + 1 + AHEAD)
                attn_out(l, 1)
                out_of(l, "yr0", 1, yg[:, 2:4, :].rearrange("p k s -> p (k s)"), ACT.Gelu_apprx_tanh)
                probs_back(l, 2)
                exponentials(l, exponentials_of[2])
                split_to(l, FIRST_HALF["yr1"] + AHEAD)
                attn_out(l, 2)
                out_of(l, "yr1", 0, yg[:, 4:6, :].rearrange("p k s -> p (k s)"), ACT.Gelu_apprx_tanh)
                probs_back(l, 3)
                split_to(l, FIRST_HALF["yr1"] + 1 + AHEAD)
                attn_out(l, 3)
                out_of(l, "yr1", 1, yg[:, 6:8, :].rearrange("p k s -> p (k s)"), ACT.Gelu_apprx_tanh)
                for i in range(2 * RNN_BLOCKS):
                    split_to(l, FIRST_HALF["rg0"] + i // 2 + AHEAD)
                    gate_curves(l, i)
                    if i + 2 < 2 * RNN_BLOCKS:
                        conv_base(l, i + 2)
                        conv_hi(l, i + 2)
                    if i % 2 == 1:
                        root(l, i // 2)
                    if i >= 5 and i % 2 == 1:
                        rnn_out(l, (i - 5) // 2)
                act.wait_ge(s_conv_step, value("conv_step", l, PER["conv_step"]))
                for name, dst, c in (("ga0", ga, 0), ("ga1", ga, 1), ("gr0", gr, 0), ("gr1", gr, 1)):
                    split_to(l, FIRST_HALF[name] + 1 + AHEAD)
                    for t in range(TT):
                        out_of(l, name, t, dst[:, t, 512 * c:512 * c + 512], ACT.Tanh, 0.5)
                split_to(l, FIRST_HALF["pr1"] + 1 + AHEAD)
                act.wait_ge(s_p_turned, value("p_turned", l, 1))
                nc.scalar.activation(r_hi[:, 0:2, :].rearrange("p k s -> p (k s)"), misc[:, 0, :], ACT.Copy,
                                     scale=1.0).then_inc(s_p_hi, 1)
                x_parts(l, 1, [(t, c) for c in range(2) for t in range(TT)], 0.5)
                split_to(l, FIRST_HALF["wo1"] + 1 + AHEAD)
                for c in range(2):
                    split_to(l, FIRST_HALF["ple"] + c + AHEAD)
                    for t in range(TT):
                        out_of(l, "ple", (c, t), ga[:, t, 512 * c:512 * c + 512], ACT.Copy, 0.5)
                x_parts(l, 2, [(t, c) for t in range(TT) for c in range(2)], 1.0)
                for j in range(FF_GROUPS):
                    for hh in range(2):
                        split_to(l, FIRST_HALF[f"g{j}"] + hh + AHEAD)
                        gate_base(l, j, hh)
                    for hh in range(2):
                        split_to(l, FIRST_HALF[f"v{j}"] + hh + AHEAD)
                        gelu(l, j, hh)
                        hidden_hi(l, j, hh)
                    if j:
                        split_to(l, FIRST_HALF[f"d{j - 1}"] + 1 + AHEAD)
                for c in range(2):
                    split_to(l, FIRST_HALF[f"pg{c}"] + 1 + AHEAD)
                    for t in range(TT):
                        out_of(l, f"pg{c}", t, gr[:, t, 512 * c:512 * c + 512], ACT.Tanh, 0.5)
                split_to(l, len(HALVES) - 1)

        @block.vector
        def _(dve):
            def split_lo(l, n):
                dve.wait_ge(s_hi_part, value("hi_part", l, n + 1))
                size = half_size(n)
                hi = w_hi[:, n % W_SLOTS, 0:size].bitcast(F32)
                nc.vector.tensor_tensor(w_lo[:, n % W_SLOTS, 0:size], raw[:, n % RAW_SLOTS, 0:size], hi,
                                        ALU.subtract).then_inc(s_split, 1)

            split = [0]

            def split_to(l, n):
                while split[0] <= min(n, len(HALVES) - 1):
                    split_lo(l, split[0])
                    split[0] += 1

            def norm(l, n, inputs):
                dve.wait_ge(s_lnp, 32 * l + 16 * n + 16)
                for t in range(TT):
                    def step(k, n=n, t=t):
                        dve.wait_ge(s_ln_step, value("ln_step", l, (TT * n + t) * LN_STEPS + k))

                    inputs(t)
                    for c in range(2):
                        nc.vector.bn_stats(st[:, t, c, :], h[:, t, 512 * c:512 * c + 512]).then_inc(s_ln_step, 1)
                    step(2)
                    nc.vector.memset(mv[:, t, 6:7], 0.0)
                    nc.vector.bn_aggr(mv[:, t, 0:2], st[:, t]).then_inc(s_ln_step, 1)
                    step(3)
                    mean, var = mv[:, t, 0:1], mv[:, t, 1:2]
                    var_eps, nhalf, y, u = (mv[:, t, i:i + 1] for i in range(2, 6))
                    nc.vector.tensor_scalar(var_eps, var, LN_EPS, None, ALU.add).then_inc(s_ln_step, 1)
                    nc.vector.tensor_scalar(nhalf, var, LN_EPS, -0.5, ALU.add, ALU.mult).then_inc(s_ln_step, 1)
                    step(4)
                    nc.vector.tensor_scalar(y.bitcast(I32), var_eps.bitcast(I32), -0.5, RSQRT_MAGIC,
                                            ALU.mult, ALU.add).then_inc(s_ln_step, 1)
                    for i in range(3):
                        step(6 + 2 * i)
                        nc.vector.scalar_tensor_tensor(out=u, in0=y, scalar=y, in1=nhalf, op0=ALU.mult,
                                                       op1=ALU.mult).then_inc(s_ln_step, 1)
                        step(7 + 2 * i)
                        nc.vector.scalar_tensor_tensor(out=y, in0=u, scalar=1.5, in1=y, op0=ALU.add,
                                                       op1=ALU.mult).then_inc(s_ln_step, 1)
                    nc.vector.scalar_tensor_tensor(out=h[:, t, :], in0=h[:, t, :], scalar=mean, in1=lnp[:, 0, :],
                                                   op0=ALU.subtract, op1=ALU.mult).then_inc(s_ln_step, 1)
                    step(13)
                    nc.vector.scalar_tensor_tensor(out=h[:, t, :], in0=h[:, t, :], scalar=y, in1=lnp[:, 1, :],
                                                   op0=ALU.mult, op1=ALU.add).then_inc(s_ln_norm, 1)

            def x_parts(l, kind, order, scale):
                for i, (t, c) in enumerate(order):
                    dve.wait_ge(s_x_hi, value("x_hi", l, 4 * kind + i + 1))
                    nc.vector.scalar_tensor_tensor(
                        out=x_lo[:, 4 * c:4 * c + 4, t * P:(t + 1) * P],
                        in0=misc[:, 2 * t + c, :].rearrange("p (k t) -> p k t", k=4), scalar=scale,
                        in1=x_hi[:, 4 * c:4 * c + 4, t * P:(t + 1) * P].bitcast(F32),
                        op0=ALU.mult, op1=ALU.subtract).then_inc(s_x_ready, 1)

            def params(l):
                dve.wait_ge(s_small, 32 * l + 32)
                lam = rnnp[:, :, :, 7]
                neg_abs, e, z, z2, poly, low = (lam_t[:, i] for i in range(6))
                nc.vector.scalar_tensor_tensor(out=neg_abs, in0=lam, scalar=-1.0, in1=lam, op0=ALU.mult,
                                               op1=ALU.min).then_inc(s_param_step, 1)
                nc.vector.tensor_scalar(rnnd[:, 0], rnnp[:, :, :, 5], 0.5, None, ALU.mult)
                nc.vector.tensor_scalar(rnnd[:, 1], rnnp[:, :, :, 6], 0.5, None, ALU.mult)
                nc.vector.tensor_scalar(nsink[:], sink[:], -1.0, None, ALU.mult)
                nc.vector.tensor_scalar(low, lam, 0.0, 4.0, ALU.min, ALU.mult).then_inc(s_param_step, 1)
                dve.wait_ge(s_param_exp, value("param_exp", l, 1))
                nc.vector.tensor_scalar(z2, e, 2.0, None, ALU.add).then_inc(s_param_step, 1)
                dve.wait_ge(s_param_step, value("param_step", l, 3))
                nc.vector.reciprocal(z2, z2).then_inc(s_param_step, 1)
                dve.wait_ge(s_param_step, value("param_step", l, 4))
                nc.vector.tensor_tensor(z, e, z2, ALU.mult).then_inc(s_param_step, 1)
                dve.wait_ge(s_param_step, value("param_step", l, 5))
                nc.vector.tensor_tensor(z2, z, z, ALU.mult).then_inc(s_param_step, 1)
                dve.wait_ge(s_param_step, value("param_step", l, 6))
                nc.vector.tensor_scalar(poly, z2, 1.0 / 15.0, None, ALU.mult).then_inc(s_param_step, 1)
                for i, k in enumerate((13, 11, 9, 7, 5, 3)):
                    dve.wait_ge(s_param_step, value("param_step", l, 7 + i))
                    nc.vector.scalar_tensor_tensor(out=poly, in0=poly, scalar=1.0 / k, in1=z2, op0=ALU.add,
                                                   op1=ALU.mult).then_inc(s_param_step, 1)
                dve.wait_ge(s_param_step, value("param_step", l, 13))
                nc.vector.scalar_tensor_tensor(out=poly, in0=poly, scalar=1.0, in1=z, op0=ALU.add,
                                               op1=ALU.mult).then_inc(s_param_step, 1)
                dve.wait_ge(s_param_step, value("param_step", l, 14))
                nc.vector.scalar_tensor_tensor(out=coef[:, 1], in0=poly, scalar=-8.0, in1=low, op0=ALU.mult,
                                               op1=ALU.add).then_inc(s_param_step, 1)
                dve.wait_ge(s_param_step, value("param_step", l, 15))
                nc.vector.tensor_scalar(coef[:, 0], coef[:, 1], -1.0, None, ALU.mult).then_inc(s_param_step, 1)

            def rotate(l):
                all_emptied(dve, l, [(name, t) for name in ("q0", "q1", "kv") for t in range(TT)])
                x1, x2 = qk[:, :, :, 0:ROPE_HALF], qk[:, :, :, ROPE_HALF:ROPE_DIM]
                cos, sin = (rope[:, i].unsqueeze(2).broadcast_to((P, TT, QK_HEADS, ROPE_HALF)) for i in range(2))
                for i, (x, c) in enumerate(((x1, cos), (x2, sin), (x2, cos), (x1, sin))):
                    nc.vector.tensor_tensor(rope_t[:, i], x, c, ALU.mult).then_inc(s_rope_step, 1)
                dve.wait_ge(s_rope_step, value("rope_step", l, 4))
                nc.vector.tensor_tensor(x1, rope_t[:, 0], rope_t[:, 1], ALU.subtract).then_inc(s_rope_step, 1)
                nc.vector.tensor_tensor(x2, rope_t[:, 2], rope_t[:, 3], ALU.add).then_inc(s_rope_step, 1)

            def softmax_max(l, r):
                g, b = divmod(r, TT)
                dve.wait_ge(s_scores, value("scores", l, r + 1))
                logits = misc[:, 0:2, :].rearrange("p a (i s) -> p (a i) s", i=2)
                other = logits[:, :, (1 - b) * P:(2 - b) * P]
                mask = masks[:, b, :].unsqueeze(1).broadcast_to((P, GROUP, P))
                nc.vector.tensor_tensor(other, other, mask, ALU.add).then_inc(s_soft_step, 1)
                dve.wait_ge(s_soft_step, value("soft_step", l, 6 * r + 1))
                nc.vector.tensor_reduce(sm[:, 0, :], logits, AX_X, ALU.max).then_inc(s_soft_step, 1)
                dve.wait_ge(s_soft_step, value("soft_step", l, 6 * r + 2))
                if r:
                    dve.wait_ge(s_exp_done, value("exp_done", l, 5 * r))
                heads = slice(GROUP * g, GROUP * (g + 1))
                nc.vector.scalar_tensor_tensor(out=sm[:, 1, :], in0=sm[:, 0, :], scalar=-SCALE, in1=nsink[:, heads],
                                               op0=ALU.mult, op1=ALU.min).then_inc(s_soft_step, 1)
                dve.wait_ge(s_soft_step, value("soft_step", l, 6 * r + 3))
                nc.vector.tensor_tensor(sm[:, 2, :], sm[:, 1, :], sink[:, heads], ALU.add).then_inc(s_soft_step, 1)

            def softmax_norm(l, r):
                dve.wait_ge(s_exp_done, value("exp_done", l, 5 * r + 5))
                nc.vector.tensor_tensor(sm[:, 5, :], sm[:, 3, :], sm[:, 4, :], ALU.add).then_inc(s_soft_step, 1)
                dve.wait_ge(s_soft_step, value("soft_step", l, 6 * r + 5))
                nc.vector.reciprocal(sm[:, 5, :], sm[:, 5, :]).then_inc(s_soft_step, 1)
                dve.wait_ge(s_soft_step, value("soft_step", l, 6 * r + 6))
                for i in range(GROUP):
                    last = nc.vector.tensor_scalar(soft[:, i, :], soft[:, i, :], sm[:, 5, i:i + 1], None, ALU.mult)
                last.then_inc(s_probs, 1)

            def attn_out(l, r):
                g, b = divmod(r, TT)
                at = (slice(None), slice(GROUP * g, GROUP * (g + 1)), slice(b * P, (b + 1) * P))
                dve.wait_ge(s_attn_hi, value("attn_hi", l, r + 1))
                nc.vector.tensor_tensor(a_lo[at], misc[:, 2, :].rearrange("p (i t) -> p i t", i=GROUP), a_hi[at].bitcast(F32),
                                        ALU.subtract).then_inc(s_attn_ready, 1)

            def conv(l, i):
                direction, b = divmod(i, RNN_BLOCKS)
                dve.wait_ge(s_conv_base, value("conv_base", l, i + 1))
                for k in range(1, CONV_W):
                    for j in range(2):
                        ft = 2 * b + j
                        if k > 1:
                            dve.wait_ge(s_conv_step, value("conv_step", l, 6 * i + 2 * (k - 2) + j + 1))
                        to, frm = (slice(k, SEQ), slice(0, SEQ - k)) if direction == 0 else \
                            (slice(0, SEQ - k), slice(k, SEQ))
                        nc.vector.scalar_tensor_tensor(
                            out=xc[:, i % 2, j, to], in0=xT[:, ft, frm], scalar=rnnp[:, direction, ft, k:k + 1],
                            in1=xc[:, i % 2, j, to], op0=ALU.mult, op1=ALU.add).then_inc(s_conv_step, 1)

            def conv_lo(l, i):
                b = i % RNN_BLOCKS
                dve.wait_ge(s_rin_hi, value("rin_hi", l, i + 1))
                nc.vector.tensor_tensor(r_lo[:, 2 * b:2 * b + 2, :], xc[:, i % 2], r_hi[:, 2 * b:2 * b + 2, :].bitcast(F32),
                                        ALU.subtract).then_inc(s_rin_ready, 1)

            def gate_input(l, i):
                direction, b = divmod(i, RNN_BLOCKS)
                state = hb if direction else hf
                dve.wait_ge(s_emptied[RING[(f"rg{direction}", (b, 1))][0]], read_out(l, (f"rg{direction}", (b, 1))))
                nc.vector.scalar_tensor_tensor(out=state[:, 2 * b:2 * b + 2, :], in0=tx[:, i % 2], scalar=1.0,
                                               in1=xc[:, i % 2], op0=ALU.add, op1=ALU.mult).then_inc(s_gated, 1)
                at = 2 * (b % 2)
                dve.wait_ge(s_pair_ready, value("pair_ready", l, i + 1))
                nc.vector.scalar_tensor_tensor(out=root_m[:, at:at + 2, :], in0=ta[:, i % 2], scalar=1.0,
                                               in1=root_m[:, at:at + 2, :], op0=ALU.add,
                                               op1=ALU.mult).then_inc(s_m2_done, 1)

            def scan(l, g):
                direction, c = divmod(g, 2)
                state = (hb if direction else hf)[:, 4 * c:4 * c + 4, :]
                first = SEQ - 1 if direction else 0
                dve.wait_ge(s_root, value("root", l, g + 1))
                nc.vector.memset(root_m[:, :, first:first + 1], 0.5).then_inc(s_rg_step, 1)
                nc.vector.memset(decay_a[:, :, first:first + 1], 0.0).then_inc(s_rg_step, 1)
                dve.wait_ge(s_rg_step, value("rg_step", l, 3 * g + 2))
                nc.vector.tensor_tensor(state, state, root_m, ALU.mult).then_inc(s_rg_step, 1)
                dve.wait_ge(s_rg_step, value("rg_step", l, 3 * g + 3))
                flat = state.rearrange("p k s -> p (k s)")
                decays = decay_a[:, :, :].rearrange("p k s -> p (k s)")
                if direction:
                    flat, decays = flat[:, ::-1], decays[:, ::-1]
                nc.vector.tensor_tensor_scan(flat, decays, flat, 0.0, ALU.mult, ALU.add).then_inc(s_scanned, 1)

            def rnn_out(l, c):
                at = slice(4 * c, 4 * c + 4)
                dve.wait_ge(s_scanned, value("scanned", l, 3 + c))
                nc.vector.tensor_tensor(hf[:, at, :], hf[:, at, :], hb[:, at, :], ALU.add).then_inc(s_rnn_step, 1)
                if c == 0:
                    all_emptied(dve, l, [(name, hh) for name in ("yr0", "yr1") for hh in range(2)])
                dve.wait_ge(s_rnn_step, value("rnn_step", l, 2 * c + 1))
                nc.vector.tensor_tensor(hf[:, at, :], hf[:, at, :], yg[:, at, :], ALU.mult).then_inc(s_rnn_step, 1)

            def rnn_lo(l, c):
                at = slice(4 * c, 4 * c + 4)
                dve.wait_ge(s_rnn_hi, value("rnn_hi", l, c + 1))
                nc.vector.tensor_tensor(r_lo[:, at, :], hf[:, at, :], r_hi[:, at, :].bitcast(F32),
                                        ALU.subtract).then_inc(s_rnn_ready, 1)

            def gated_projection(l, name, gate, c, t):
                key = (name, t)
                dve.wait_ge(s_products, made(l, name, t))
                at = gate[:, t, 512 * c:512 * c + 512]
                nc.vector.scalar_tensor_tensor(out=at, in0=at, scalar=1.0, in1=bank_of(key), op0=ALU.add,
                                               op1=ALU.mult).then_inc(s_emptied[RING[key][0]], 1)

            def outer_taps(l, j, hh):
                dve.wait_ge(s_gate_base, value("gate_base", l, 2 * j + hh + 1))
                c = tmp[:, hh + 2 * (j % 2)]
                bank = bank_of((f"g{j}", hh))
                for d in range(2):
                    ft = 4 * j + 2 * hh + d
                    nc.vector.scalar_tensor_tensor(
                        out=c[:, d, 1:SEQ], in0=bank[:, SEQ * d:SEQ * (d + 1) - 1], scalar=ffnp[:, ft, 0:1],
                        in1=c[:, d, 1:SEQ], op0=ALU.mult, op1=ALU.add).then_inc(s_tap_step, 1)
                for d in range(2):
                    ft = 4 * j + 2 * hh + d
                    dve.wait_ge(s_tap_step, value("tap_step", l, 4 * j + 2 * hh + d + 1))
                    last = nc.vector.scalar_tensor_tensor(
                        out=c[:, d, 0:SEQ - 1], in0=bank[:, SEQ * d + 1:SEQ * (d + 1)], scalar=ffnp[:, ft, 2:3],
                        in1=c[:, d, 0:SEQ - 1], op0=ALU.mult, op1=ALU.add)
                last.then_inc(s_emptied[RING[f"g{j}", hh][0]], 1)

            def hidden(l, j, hh):
                key = (f"v{j}", hh)
                dve.wait_ge(s_products, made(l, *key))
                dve.wait_ge(s_gelu, value("gelu", l, 2 * j + hh + 1))
                c = tmp[:, hh + 2 * (j % 2)]
                nc.vector.tensor_tensor(c, c, bank_of(key).rearrange("p (d s) -> p d s", d=2), ALU.mult).then_inc(
                    s_emptied[RING[key][0]], 1)

            def hidden_lo(l, j, hh):
                dve.wait_ge(s_f_hi, value("f_hi", l, 2 * j + hh + 1))
                at = slice(4 * (j % 2) + 2 * hh, 4 * (j % 2) + 2 * hh + 2)
                nc.vector.tensor_tensor(a_lo[:, at, :], tmp[:, hh + 2 * (j % 2)], a_hi[:, at, :].bitcast(F32),
                                        ALU.subtract).then_inc(s_f_ready, 1)

            for begin in (s_split, s_ln_norm, s_rnn_ready, s_f_ready, s_gated, s_m2_done, s_scanned, s_tail_step,
                          *s_emptied):
                dve.sem_inc(begin, 1)
            dve.wait_ge(s_h, 32)
            dve.wait_ge(s_rope, 16)
            with dve.Fori(0, DEPTH) as l:
                split[0] = 0
                split_to(l, 0)
                norm(l, 0, lambda t: dve.wait_ge(s_tail_step, value("tail_step", l, 0)))
                split_to(l, 2)
                x_parts(l, 0, [(t, c) for t in range(TT) for c in range(2)], 1.0)
                params(l)
                split_to(l, FIRST_HALF["kv"] + 1 + AHEAD)
                rotate(l)
                split_to(l, FIRST_HALF["xr1"] + AHEAD)
                conv(l, 0)
                conv_lo(l, 0)
                softmax_max(l, 0)
                split_to(l, FIRST_HALF["xr1"] + 1 + AHEAD)
                conv(l, 1)
                softmax_norm(l, 0)
                conv_lo(l, 1)
                softmax_max(l, 1)
                split_to(l, FIRST_HALF["yr0"] + AHEAD)
                attn_out(l, 0)
                softmax_norm(l, 1)
                softmax_max(l, 2)
                split_to(l, FIRST_HALF["yr0"] + 1 + AHEAD)
                attn_out(l, 1)
                softmax_norm(l, 2)
                softmax_max(l, 3)
                split_to(l, FIRST_HALF["yr1"] + AHEAD)
                attn_out(l, 2)
                softmax_norm(l, 3)
                split_to(l, FIRST_HALF["yr1"] + 1 + AHEAD)
                attn_out(l, 3)
                for i in range(2 * RNN_BLOCKS):
                    split_to(l, FIRST_HALF["rg0"] + i // 2 + AHEAD)
                    gate_input(l, i)
                    if i + 2 < 2 * RNN_BLOCKS:
                        conv(l, i + 2)
                        conv_lo(l, i + 2)
                    if i % 2 == 1:
                        scan(l, i // 2)
                    if i >= 5 and i % 2 == 1:
                        rnn_out(l, (i - 5) // 2)
                        rnn_lo(l, (i - 5) // 2)
                split_to(l, FIRST_HALF["pa0"] + 1 + AHEAD)
                for c in range(2):
                    split_to(l, FIRST_HALF[f"pa{c}"] + 1 + AHEAD)
                    for t in range(TT):
                        if c == 0 and t == 0:
                            all_emptied(dve, l, [(name, i) for name in ("ga0", "ga1") for i in range(TT)])
                        gated_projection(l, f"pa{c}", ga, c, t)
                for c in range(2):
                    split_to(l, FIRST_HALF[f"pr{c}"] + 1 + AHEAD)
                    for t in range(TT):
                        if c == 0 and t == 0:
                            all_emptied(dve, l, [(name, i) for name in ("gr0", "gr1") for i in range(TT)])
                        gated_projection(l, f"pr{c}", gr, c, t)
                    all_emptied(dve, l, [(f"pr{c}", t) for t in range(TT)])
                    for t in range(TT):
                        at = (slice(None), t, slice(512 * c, 512 * c + 512))
                        nc.vector.tensor_tensor(ga[at], ga[at], gr[at], ALU.add).then_inc(s_merge, 1)
                dve.wait_ge(s_p_hi, value("p_hi", l, 1))
                nc.vector.tensor_tensor(r_lo[:, 0:2, :].rearrange("p k s -> p (k s)"), misc[:, 0, :], r_hi[:, 0:2, :].rearrange("p k s -> p (k s)").bitcast(F32),
                                        ALU.subtract).then_inc(s_p_ready, 1)
                x_parts(l, 1, [(t, c) for c in range(2) for t in range(TT)], 0.5)
                for c in range(2):
                    split_to(l, FIRST_HALF[f"wo{c}"] + 1 + AHEAD)
                    for t in range(TT):
                        key = (f"wo{c}", t)
                        dve.wait_ge(s_products, made(l, *key))
                        at = h[:, t, 512 * c:512 * c + 512]
                        nc.vector.scalar_tensor_tensor(out=at, in0=at, scalar=ALPHA, in1=bank_of(key), op0=ALU.mult,
                                                       op1=ALU.add).then_inc(s_emptied[RING[key][0]], 1)
                norm(l, 1, lambda t: all_emptied(dve, l, [("wo0", t), ("wo1", t)]))
                split_to(l, FIRST_HALF["ple"] + 1 + AHEAD)
                x_parts(l, 2, [(t, c) for t in range(TT) for c in range(2)], 1.0)
                for j in range(FF_GROUPS):
                    for hh in range(2):
                        split_to(l, FIRST_HALF[f"g{j}"] + hh + AHEAD)
                        outer_taps(l, j, hh)
                    for hh in range(2):
                        split_to(l, FIRST_HALF[f"v{j}"] + hh + AHEAD)
                        hidden(l, j, hh)
                        hidden_lo(l, j, hh)
                    if j:
                        split_to(l, FIRST_HALF[f"d{j - 1}"] + 1 + AHEAD)
                for c in range(2):
                    split_to(l, FIRST_HALF[f"pg{c}"] + 1 + AHEAD)
                all_emptied(dve, l, [(f"pg{c}", t) for c in range(2) for t in range(TT)]
                            + [("ple", (c, t)) for c in range(2) for t in range(TT)])
                flat = ga[:, :, :].rearrange("p t n -> p (t n)")
                h_flat = h[:, :, :].rearrange("p t n -> p (t n)")
                nc.vector.scalar_tensor_tensor(out=flat, in0=gr.rearrange("p t n -> p (t n)"), scalar=1.0, in1=flat,
                                               op0=ALU.add, op1=ALU.mult).then_inc(s_tail_step, 1)
                dve.wait_ge(s_tail_step, value("tail_step", l, 1))
                nc.vector.scalar_tensor_tensor(out=h_flat, in0=h_flat, scalar=ALPHA, in1=flat, op0=ALU.mult,
                                               op1=ALU.add).then_inc(s_tail_step, 1)
                dve.wait_ge(s_tail_step, value("tail_step", l, 2))
                for t in range(TT):
                    dve.wait_ge(s_products, made(l, f"d{FF_GROUPS - 1}", t))
                    nc.vector.tensor_tensor(h[:, t, :], h[:, t, :], misc[:, 2 * t:2 * t + 2, :].rearrange(
                        "p a n -> p (a n)"), ALU.add).then_inc(s_tail_step, 1)
            norm(DEPTH, 0, lambda t: dve.wait_ge(s_tail_step, value("tail_step", DEPTH, 0)))


def rope_tables():
    pos = np.arange(SEQ, dtype=np.float32)
    inv = np.float32(ROPE_THETA) ** (-np.arange(0, ROPE_DIM, 2, dtype=np.float32) / np.float32(ROPE_DIM))
    ang = pos[:, None] * inv[None, :].astype(np.float32)
    both = np.stack([np.cos(ang), np.sin(ang)]).astype(np.float32)
    return np.ascontiguousarray(both.reshape(2, TT, P, ROPE_HALF).transpose(2, 0, 1, 3))


_AS_THEY_COME = ["x", "p", "w_in", "attn_sink", "rg_w_a", "rg_w_x", "w_proj_attn", "w_proj_rnn", "w_out",
                 "w_up", "w_down", "w_ple", "w_ple_gate"]


def kernel(**inputs):
    import concourse.bacc as bacc
    from concourse.bass_utils import run_bass_kernel_spmd

    given = {k: np.asarray(x) for k, x in inputs.items()}
    laid = {k: given[k] for k in _AS_THEY_COME}
    gains, offsets = [given["ln_in_g"]], [given["ln_in_b"]]
    for i in range(DEPTH):
        gains += [given["ln1_g"][i], given["ln2_g"][i]]
        offsets += [given["ln1_b"][i], given["ln2_b"][i]]
    laid["ln"] = np.stack([np.stack(gains), np.stack(offsets)], axis=1)
    rnn = np.concatenate([given["rnn_conv_w"]] + [given[k][:, :, None] for k in
                         ("rnn_conv_b", "rg_b_a", "rg_b_x", "rg_lambda")], axis=2)
    laid["rnnp"] = rnn.reshape(DEPTH, 2, 8, KT, P).transpose(0, 4, 1, 3, 2)
    ffn = np.concatenate([given["ffn_conv_w"], given["ffn_conv_b"][:, None]], axis=1)
    laid["ffnp"] = ffn.reshape(DEPTH, 4, FF_TILES, P).transpose(0, 3, 2, 1)
    laid["rope"] = rope_tables()

    nc = bacc.Bacc("TRN2", target_bir_lowering=False, num_devices=1)
    arrays, aps = {}, {}
    for name, x in laid.items():
        arrays[f"in_{name}_dram"] = np.ascontiguousarray(x)
        aps[name] = nc.dram_tensor(f"in_{name}_dram", x.shape, F32, kind="ExternalInput").ap()
    out = nc.dram_tensor("out_0_dram", (1, SEQ, D), F32, kind="ExternalOutput").ap()
    hybrid_encoder(nc, aps, out)
    r = run_bass_kernel_spmd(nc, [arrays], core_ids=[0])
    return r.results[0]["out_0_dram"]
```

```python
from contextlib import ExitStack

import numpy as np

import concourse.bass as bass
from concourse import mybir

F32 = mybir.dt.float32
F32R = mybir.dt.float32r
I32 = mybir.dt.int32
ALU = mybir.AluOpType
ACT = mybir.ActivationFunctionType
AX_X = mybir.AxisListType.X

P = 128
DEPTH, SEQ, D = 2, 256, 1024
HEADS, KV_HEADS, HEAD_DIM = 8, 2, 128
GROUP = HEADS // KV_HEADS
QK_HEADS = HEADS + KV_HEADS
ROPE_DIM = HEAD_DIM // 4
ROPE_HALF = ROPE_DIM // 2
ROPE_THETA = 500000.0
KV_WIDTH = KV_HEADS * HEAD_DIM
TT = SEQ // P
KT = D // P
RNN_BLOCKS, BLOCK_W = 4, 256
CONV_W = 4
D_FF = 3 * D
FF_TILES = D_FF // P
FF_GROUPS = D_FF // 512
LAST = FF_GROUPS - 1
D_PLE = 256
LN_EPS = 1e-5
ALPHA = float((2 * DEPTH) ** 0.25)
SCALE = float(HEAD_DIM) ** -0.5
MASKED = -1e30
RSQRT_MAGIC = 1597463007.0

Q0 = 0
K0 = HEADS * HEAD_DIM
XR0 = K0 + 2 * KV_WIDTH
YR0 = XR0 + D
GA0 = YR0 + D
GR0 = GA0 + D

UNITS = {
    "q0": ("token", "w_in", Q0), "q1": ("token", "w_in", Q0 + 512), "kv": ("token", "w_in", K0),
    "xr0": ("feature", "w_in", XR0), "xr1": ("feature", "w_in", XR0 + 512),
    "yr0": ("feature", "w_in", YR0), "yr1": ("feature", "w_in", YR0 + 512),
    "rg0": ("gates", None, 0), "rg1": ("gates", None, 1),
    "ga0": ("token", "w_in", GA0), "ga1": ("token", "w_in", GA0 + 512),
    "gr0": ("token", "w_in", GR0), "gr1": ("token", "w_in", GR0 + 512),
    "pa0": ("token", "w_proj_attn", 0), "pa1": ("token", "w_proj_attn", 512),
    "pr0": ("token", "w_proj_rnn", 0), "pr1": ("token", "w_proj_rnn", 512),
    "wo0": ("token", "w_out", 0), "wo1": ("token", "w_out", 512),
    "ple": ("ple", "w_ple", 0),
    "pg0": ("token", "w_ple_gate", 0), "pg1": ("token", "w_ple_gate", 512),
}
for _j in range(FF_GROUPS):
    UNITS[f"g{_j}"] = ("feature", "w_up", 512 * _j)
    UNITS[f"v{_j}"] = ("feature", "w_up", D_FF + 512 * _j)
    UNITS[f"d{_j}"] = ("down", "w_down", _j)
BY_TILE = ("q0", "wo1", "pg0", f"d{LAST}")
WITH_BLOCK = ("xr1", "q1", "kv", "ga0", "ga1", "gr0", "gr1", "yr0")

ORDER = ["q0", "xr0", "xr1", "q1", "kv", "ga0", "ga1", "gr0", "gr1", "yr0", "yr1", "pa0", "pa1", "pr0", "pr1",
         "wo0", "wo1", "ple", "pg0", "g0", "v0"]
for _j in range(1, LAST):
    ORDER += [f"g{_j}", f"v{_j}", f"d{_j - 1}"]
ORDER += [f"g{LAST}", f"v{LAST}", "pg1", f"d{LAST - 1}", f"d{LAST}"]
ITEMS = []
for _name in ORDER:
    ITEMS.append((_name, 0))
    if _name in WITH_BLOCK:
        _i = WITH_BLOCK.index(_name)
        ITEMS.append((f"rg{_i // RNN_BLOCKS}", _i % RNN_BLOCKS))
    if _name != "ple":
        ITEMS.append((_name, 1))
    if _name == "pg0":
        ITEMS.append(("ple", 1))
ITEM = {item: n for n, item in enumerate(ITEMS)}
W_SLOTS = 3
RAW_SLOTS = 3
AHEAD = 2
assert len(ITEMS) % W_SLOTS == 0 and len(ITEMS) % RAW_SLOTS == 0


def kind_of(n):
    return UNITS[ITEMS[n][0]][0]


def item_size(n):
    return 1024 if kind_of(n) in ("gates", "ple") else 2048


def item_loads(n):
    return 2 if kind_of(n) == "gates" else 1


LOADED = []
_at = [0] * RAW_SLOTS
for _n in range(len(ITEMS)):
    _at[_n % RAW_SLOTS] += 16 * item_loads(_n)
    LOADED.append(_at[_n % RAW_SLOTS])
LOADED_PER_LAYER = list(_at)

PRODUCT = {}
AFTER_ITEM = [0] * len(ITEMS)
_c = 0
for _n, (_name, _part) in enumerate(ITEMS):
    _kind = kind_of(_n)
    if (_name, _part) == ("ple", 1):
        _parts = []
    elif _name == f"d{LAST}":
        _parts = [] if _part == 0 else [(0, 0), (0, 1), (1, 0), "half", (1, 1)]
    elif _name in BY_TILE:
        _parts = [] if _part == 0 else [0, "half", 1]
    elif _kind in ("token", "down"):
        _parts = ["half"] if _part == 0 else [0, 1]
    elif _kind == "feature":
        _parts = [_part]
    elif _kind == "gates":
        _parts = [(_part, g) for g in range(2)]
    else:
        _parts = [(_part, t) for t in range(TT)]
    for _p in _parts:
        _c += 1
        PRODUCT[_name, _p] = _c
        if (_name, _p) == ("pg0", 0):
            for _t in range(TT):
                _c += 1
                PRODUCT["ple", (1, _t)] = _c
    AFTER_ITEM[_n] = _c
    if _name in BY_TILE and _part == 1:
        AFTER_ITEM[_n - 1] = PRODUCT[_name, "half"]
    if (_name, _part) == ("ple", 1):
        AFTER_ITEM[_n] = PRODUCT["ple", (1, TT - 1)]

RING = {}
_uses = [0] * 4
_touched = [-1, -2]
_open = {}
for _n, (_name, _part) in enumerate(ITEMS):
    _kind = kind_of(_n)
    if _kind == "down":
        continue
    if _kind in ("gates", "ple") or _part == 0:
        _open[_name] = _touched.index(min(_touched))
        for _b in range(2):
            _bank = 2 * _open[_name] + _b
            RING[_name, (_part, _b) if _kind in ("gates", "ple") else _b] = (_bank, _uses[_bank])
            _uses[_bank] += 1
    _touched[_open[_name]] = _n
RING_USES = list(_uses)

GROUPS = 2 * RNN_BLOCKS // 2
ROUNDS = KV_HEADS * TT
LN_REST = 12
LN_STEPS = 2 + LN_REST
STATS_DONE = ((2, LN_STEPS + 2), (2 * LN_STEPS + 3, 2 * LN_STEPS + 3 + LN_REST + 1))
PER = dict(
    split=len(ITEMS), hi_part=len(ITEMS), products=AFTER_ITEM[-1],
    ln_step=2 * TT * LN_STEPS, ln_norm=4 * TT, x_turned=3 * 4, x_hi=3 * 4, x_ready=3 * 4,
    rope_step=6, qk_turned=5, qk_ready=5,
    scores=ROUNDS, soft_step=6 * ROUNDS, exp_done=5 * ROUNDS, probs=ROUNDS, probs_turned=ROUNDS,
    probs_back=ROUNDS, mixed=ROUNDS, attn_hi=ROUNDS, attn_ready=ROUNDS,
    param_step=16, param_exp=1, conv_base=8, conv_step=48, rin_hi=8, rin_ready=8,
    decay=16, pair_ready=8, m2_done=8, gated=8, root=GROUPS, rg_step=3 * GROUPS, scanned=GROUPS,
    rnn_step=4, rnn_hi=2, rnn_ready=2, merge=4, p_turned=1, p_hi=1, p_ready=1,
    gate_base=12, tap_step=24, gelu=12, f_hi=12, f_ready=12, added=2 * TT, ple_step=2,
)


BASE = {name: 1 for name in ["p_turned", "ln_norm", "rnn_ready", "f_ready", "gated", "m2_done", "scanned",
                             "ple_step"]}
BASE["split"] = RAW_SLOTS
BASE["products"] = PER["products"] + 1 - min(AFTER_ITEM[-W_SLOTS], PRODUCT[f"d{LAST}", (0, 0)])


def hybrid_encoder(nc, a, out):
    with ExitStack() as ctx:
        def sb(name, shape, dt=F32):
            return ctx.enter_context(nc.sbuf_tensor("sb_" + name, shape, dt))

        def sem(name):
            return ctx.enter_context(nc.semaphore(name))

        w_hi = sb("w_hi", [P, W_SLOTS, 2048], F32R)
        w_lo = sb("w_lo", [P, W_SLOTS, 2048], F32R)
        x_hi = sb("x_hi", [P, KT, SEQ], F32R)
        x_lo = sb("x_lo", [P, KT, SEQ], F32R)
        a_hi = sb("a_hi", [P, KT, SEQ], F32R)
        a_lo = sb("a_lo", [P, KT, SEQ], F32R)
        r_hi = sb("r_hi", [P, KT, SEQ], F32R)
        r_lo = sb("r_lo", [P, KT, SEQ], F32R)

        raw = sb("raw", [P, RAW_SLOTS, 2048])
        h = sb("h", [P, TT, D])
        lnp = sb("lnp", [P, 2, D])
        qk = sb("qk", [P, TT, QK_HEADS, HEAD_DIM])
        v = sb("v", [P, TT, KV_HEADS, HEAD_DIM])
        qkT = sb("qkT", [P, QK_HEADS, SEQ])
        yg = qk[:, :, :, :].rearrange("p t h d -> p (t h d)")[:, 0:KT * SEQ].rearrange(
            "p (k s) -> p k s", k=KT)
        hf = lnp[:, :, :].rearrange("p i (k s) -> p (i k) s", s=SEQ)
        hb = sb("hb", [P, KT, SEQ])
        xT = sb("xT", [P, KT, SEQ])
        ga = sb("ga", [P, TT, D])
        gr = xT[:, :, :].rearrange("p (t a) s -> p t (a s)", t=TT)
        soft = sb("soft", [P, GROUP, SEQ])
        pT = sb("pT", [P, TT, GROUP, P])
        decay_a = sb("decay_a", [P, 4, SEQ])
        root_m = sb("root_m", [P, 4, SEQ])
        tmp = sb("tmp", [P, 6, 2, SEQ])
        xc, ta, tx = tmp[:, 0:2], tmp[:, 2:4], tmp[:, 4:6]
        p_in = sb("p_in", [P, TT, D_PLE])
        rnnp = sb("rnnp", [P, 2, KT, 8])
        rnnd = sb("rnnd", [P, 2, 2, KT])
        coef = sb("coef", [P, 2, 2, KT])
        lam_t = sb("lam_t", [P, 6, 2, KT])
        ffnp = sb("ffnp", [P, FF_TILES, 4])
        sink = sb("sink", [P, HEADS])
        nsink = sb("nsink", [P, HEADS])
        rope = sb("rope", [P, 2, TT, ROPE_HALF])
        rope_size = TT * QK_HEADS * ROPE_HALF
        rope_t = [buf.rearrange("p (i t h c) -> p i t h c", i=2, t=TT, h=QK_HEADS)
                  for buf in (soft[:, :, :].rearrange("p i s -> p (i s)")[:, 0:2 * rope_size],
                              pT[:, :, :, :].rearrange("p a g t -> p (a g t)")[:, 0:2 * rope_size])]
        masks = sb("masks", [P, 2, P])
        ident = sb("ident", [P, P])
        st = sb("st", [P, TT, 2, 6])
        mv = sb("mv", [P, TT, 8])
        sm = sb("sm", [P, 6, GROUP])

        ring = ctx.enter_context(nc.psum_tensor("ring", [P, 4, 512], F32))
        misc = ctx.enter_context(nc.psum_tensor("misc", [P, 4, 512], F32))

        s_raw = [sem(f"raw_loaded{i}") for i in range(RAW_SLOTS)]
        s_emptied = [sem(f"bank_emptied{i}") for i in range(4)]
        s_split = sem("split")
        s_hi_part = sem("hi_part")
        s_products = sem("products")
        s_ln_step = sem("ln_step")
        s_ln_norm = sem("ln_norm")
        s_x_turned = sem("x_turned")
        s_x_hi = sem("x_hi")
        s_x_ready = sem("x_ready")
        s_rope_step = sem("rope_step")
        s_qk_turned = sem("qk_turned")
        s_qk_ready = sem("qk_ready")
        s_scores = sem("scores")
        s_soft_step = sem("soft_step")
        s_exp_done = sem("exp_done")
        s_probs = sem("probs")
        s_probs_turned = sem("probs_turned")
        s_probs_back = sem("probs_back")
        s_mixed = sem("mixed")
        s_attn_hi = sem("attn_hi")
        s_attn_ready = sem("attn_ready")
        s_param_step = sem("param_step")
        s_param_exp = sem("param_exp")
        s_conv_base = sem("conv_base")
        s_conv_step = sem("conv_step")
        s_rin_hi = sem("rin_hi")
        s_rin_ready = sem("rin_ready")
        s_decay = sem("decay")
        s_pair_ready = sem("pair_ready")
        s_m2_done = sem("m2_done")
        s_gated = sem("gated")
        s_root = sem("root")
        s_rg_step = sem("rg_step")
        s_scanned = sem("scanned")
        s_rnn_step = sem("rnn_step")
        s_rnn_hi = sem("rnn_hi")
        s_rnn_ready = sem("rnn_ready")
        s_merge = sem("merge")
        s_p_turned = sem("p_turned")
        s_p_hi = sem("p_hi")
        s_p_ready = sem("p_ready")
        s_gate_base = sem("gate_base")
        s_tap_step = sem("tap_step")
        s_gelu = sem("gelu")
        s_f_hi = sem("f_hi")
        s_f_ready = sem("f_ready")
        s_added = sem("added")
        s_ple_step = sem("ple_step")
        s_h = [sem(f"h_loaded{t}") for t in range(TT)]
        s_lnp = sem("lnp_loaded")
        s_small = sem("rnn_params_loaded")
        s_ffnp = sem("ffn_params_loaded")
        s_p = sem("p_loaded")
        s_const = sem("constants")
        s_rope = sem("rope_loaded")
        s_out = sem("out_stored")

        def value(name, l, count):
            return l * PER[name] + count + BASE.get(name, 0)

        def made(l, name, part):
            return value("products", l, PRODUCT[name, part])

        def read_out(l, key):
            return l * RING_USES[RING[key][0]] + RING[key][1] + 2

        def free(l, key):
            return read_out(l, key) - 1

        def all_emptied(eng, l, keys):
            latest = {}
            for key in keys:
                bank, before = RING[key]
                latest[bank] = max(latest.get(bank, 0), before + 1)
            for bank, count in latest.items():
                eng.wait_ge(s_emptied[bank], l * RING_USES[bank] + count + 1)

        def bank_of(key):
            return ring[:, RING[key][0], :]

        block = ctx.enter_context(nc.Block())

        @block.sync
        def _(sp):
            def item_source(l, n):
                name, part = ITEMS[n]
                kind, src, first = UNITS[name]
                if kind == "gates":
                    return [a[w][bass.ds(l, 1), first, part].rearrange("a (k p) d -> p (a k) d", p=P)
                            for w in ("rg_w_a", "rg_w_x")]
                view = a[src][bass.ds(l, 1)].rearrange("a (k p) n -> p (a k) n", p=P)
                if kind == "token":
                    return [view[:, 4 * part:4 * part + 4, first:first + 512]]
                if kind == "feature":
                    return [view[:, :, first + 256 * part:first + 256 * part + 256]]
                if kind == "ple":
                    return [view[:, :, 512 * part:512 * part + 512]]
                return [view[:, 4 * first + 2 * part:4 * first + 2 * part + 2, :]]

            def load_item(l, n):
                sp.wait_ge(s_split, value("split", l, n - RAW_SLOTS + 1))
                slot = n % RAW_SLOTS
                parts = item_source(l, n)
                step = item_size(n) // len(parts)
                for i, src in enumerate(parts):
                    dst = raw[:, slot, i * step:(i + 1) * step].rearrange("p (k n) -> p k n", k=src.shape[1])
                    sp.dma_start(dst, src).then_inc(s_raw[slot], 16)

            def load_norm(l, n):
                if n == 0:
                    sp.wait_ge(s_ln_norm, value("ln_norm", l, 0))
                else:
                    sp.wait_ge(s_rnn_ready, value("rnn_ready", l, 2))
                sp.dma_start(lnp[:], a["ln"][bass.ds(2 * l + n, 1)].to_broadcast((P, 2, D))).then_inc(s_lnp, 16)

            sp.dma_start(h[:, 0, :], a["x"][0, 0:P, :]).then_inc(s_h[0], 16)
            with sp.Fori(0, DEPTH) as l:
                load_item(l, 0)
                load_norm(l, 0)
                for n in range(1, W_SLOTS):
                    load_item(l, n)
                sp.wait_ge(s_rnn_ready, value("rnn_ready", l, 0))
                sp.dma_start(rnnp[:], a["rnnp"][bass.ds(l, 1)].rearrange("a p d k c -> p (a d) k c")
                             ).then_inc(s_small, 16)
                sp.dma_start(sink[:], a["attn_sink"][bass.ds(l, 1)].to_broadcast((P, HEADS))).then_inc(s_small, 16)
                sp.wait_ge(s_p_turned, value("p_turned", l, 0))
                sp.dma_start(p_in[:], a["p"][bass.ds(l, 1), 0].rearrange("a (t q) c -> q (a t) c", q=P)
                             ).then_inc(s_p, 16)
                for n in range(W_SLOTS, ITEM["gr0", 0]):
                    load_item(l, n)
                sp.wait_ge(s_f_ready, value("f_ready", l, 0))
                sp.dma_start(ffnp[:], a["ffnp"][bass.ds(l, 1)].rearrange("a p k c -> p (a k) c")
                             ).then_inc(s_ffnp, 16)
                for n in range(ITEM["gr0", 0], ITEM["wo0", 1]):
                    load_item(l, n)
                load_norm(l, 1)
                for n in range(ITEM["wo0", 1], len(ITEMS)):
                    load_item(l, n)
            sp.wait_ge(s_ln_norm, value("ln_norm", DEPTH, 0))
            sp.dma_start(lnp[:], a["ln"][2 * DEPTH:2 * DEPTH + 1].to_broadcast((P, 2, D))).then_inc(s_lnp, 16)
            for t in range(TT):
                for c in range(2):
                    at = slice(512 * c, 512 * c + 512)
                    sp.wait_ge(s_ln_norm, value("ln_norm", DEPTH, 2 * t + c + 1))
                    sp.dma_start(out[0, t * P:(t + 1) * P, at], h[:, t, at]).then_inc(s_out, 16)
            sp.wait_ge(s_out, 2 * 16 * TT)

        @block.gpsimd
        def _(pool):
            nc.gpsimd.memset(ident[:], 0.0).then_inc(s_const, 1)
            nc.gpsimd.memset(masks[:], 0.0).then_inc(s_const, 1)
            pool.wait_ge(s_const, 2)
            nc.gpsimd.affine_select(out=ident[:], in_=ident[:], compare_op=ALU.not_equal, fill=1.0, base=0,
                                    pattern=[[-1, P]], channel_multiplier=1).then_inc(s_const, 1)
            nc.gpsimd.affine_select(out=masks[:, 0, :], in_=masks[:, 0, :], compare_op=ALU.is_ge, fill=MASKED,
                                    base=0, pattern=[[-1, P]], channel_multiplier=1).then_inc(s_const, 1)
            nc.gpsimd.affine_select(out=masks[:, 1, :], in_=masks[:, 1, :], compare_op=ALU.is_ge, fill=MASKED,
                                    base=0, pattern=[[1, P]], channel_multiplier=-1).then_inc(s_const, 1)

        @block.tensor
        def _(pe):
            def three(dst, lhs, rhs, first, last):
                nc.tensor.matmul(dst, lhs[0], rhs[0], start=first, stop=False)
                nc.tensor.matmul(dst, lhs[0], rhs[1], start=False, stop=False)
                return nc.tensor.matmul(dst, lhs[1], rhs[0], start=False, stop=last)

            def weights(l, n):
                pe.wait_ge(s_split, value("split", l, n + 1))
                return n % W_SLOTS

            def token_part(l, name, hh, t, left):
                slot = weights(l, ITEM[name, hh])
                if hh == 0:
                    pe.wait_ge(s_emptied[RING[name, t][0]], free(l, (name, t)))
                for k in range(4):
                    kk = 4 * hh + k
                    cols = slice(512 * k, 512 * k + 512)
                    last = three(bank_of((name, t)), [x[:, kk, t * P:(t + 1) * P] for x in left],
                                 [w_hi[:, slot, cols], w_lo[:, slot, cols]], kk == 0, kk == KT - 1)
                return last

            def token_half(l, name, hh, left):
                tile_0 = token_part(l, name, hh, 0, left)
                if hh == 1:
                    tile_0.then_inc(s_products, 1)
                token_part(l, name, hh, 1, left).then_inc(s_products, 1)

            def feature_half(l, name, hh):
                slot = weights(l, ITEM[name, hh])
                pe.wait_ge(s_emptied[RING[name, hh][0]], free(l, (name, hh)))
                for j in range(2):
                    for k in range(KT):
                        cols = slice(256 * k + P * j, 256 * k + P * (j + 1))
                        last = three(bank_of((name, hh))[:, SEQ * j:SEQ * (j + 1)],
                                     [w_hi[:, slot, cols], w_lo[:, slot, cols]],
                                     [x_hi[:, k, :], x_lo[:, k, :]], k == 0, k == KT - 1)
                last.then_inc(s_products, 1)

            def feature_unit(l, name):
                feature_half(l, name, 0)
                feature_half(l, name, 1)

            def token_unit(l, name, left):
                token_half(l, name, 0, left)
                token_half(l, name, 1, left)

            def token_unit_by_tile(l, name, left, parts=None, after=None):
                for t in range(TT):
                    for hh in range(2):
                        if parts is not None:
                            x_ready(l, parts + 2 * t + hh + 1)
                        last = token_part(l, name, hh, t, left)
                        if (t, hh) != (0, 0):
                            last.then_inc(s_products, 1)
                    if t == 0 and after:
                        after()

            def gates_block(l, i):
                direction, b = divmod(i, RNN_BLOCKS)
                slot = weights(l, ITEM[f"rg{direction}", b])
                pe.wait_ge(s_rin_ready, value("rin_ready", l, i + 1))
                for g in range(2):
                    key = (f"rg{direction}", (b, g))
                    pe.wait_ge(s_emptied[RING[key][0]], free(l, key))
                    for d in range(2):
                        for k in range(2):
                            at = 512 * g + 256 * k + P * d
                            last = three(bank_of(key)[:, SEQ * d:SEQ * (d + 1)],
                                         [w_hi[:, slot, at:at + P], w_lo[:, slot, at:at + P]],
                                         [r_hi[:, 2 * b + k, :], r_lo[:, 2 * b + k, :]], k == 0, k == 1)
                    last.then_inc(s_products, 1)

            def ple_part(l, hh, t):
                slot = weights(l, ITEM["ple", hh])
                key = ("ple", (hh, t))
                pe.wait_ge(s_emptied[RING[key][0]], free(l, key))
                for k in range(2):
                    cols = slice(512 * k, 512 * k + 512)
                    last = three(bank_of(key), [r_hi[:, k, t * P:(t + 1) * P], r_lo[:, k, t * P:(t + 1) * P]],
                                 [w_hi[:, slot, cols], w_lo[:, slot, cols]], k == 0, k == 1)
                last.then_inc(s_products, 1)

            def q0_tile_1(l):
                turn_h(l, 0, 1)

            def pg0_tile_1(l):
                turn_h(l, 1, 1)
                ple_part(l, 1, 0)
                ple_part(l, 1, 1)

            def down_part(l, j, hh, t, halves=(0, 1)):
                slot = weights(l, ITEM[f"d{j}", hh])
                for c in halves:
                    for k in range(2):
                        cols = slice(1024 * k + 512 * c, 1024 * k + 512 * (c + 1))
                        kk = 4 * (j % 2) + 2 * hh + k
                        last = three(misc[:, 2 * t + c, :],
                                     [a_hi[:, kk, t * P:(t + 1) * P], a_lo[:, kk, t * P:(t + 1) * P]],
                                     [w_hi[:, slot, cols], w_lo[:, slot, cols]],
                                     j == 0 and hh == 0 and k == 0,
                                     j == FF_GROUPS - 1 and hh == 1 and k == 1)
                return last

            def down_unit(l, j):
                for hh in range(2):
                    pe.wait_ge(s_f_ready, value("f_ready", l, 2 * j + hh + 1))
                    tile_0 = down_part(l, j, hh, 0)
                    if hh == 1:
                        tile_0.then_inc(s_products, 1)
                    down_part(l, j, hh, 1).then_inc(s_products, 1)

            def last_down_unit(l):
                j = FF_GROUPS - 1
                pe.wait_ge(s_f_ready, value("f_ready", l, 2 * j + 2))
                for t in range(TT):
                    for c in range(2):
                        first = down_part(l, j, 0, t, [c])
                        if (t, c) == (1, 1):
                            first.then_inc(s_products, 1)
                        down_part(l, j, 1, t, [c]).then_inc(s_products, 1)

            def turn(dst, src):
                return nc.tensor.transpose(dst, src, ident[:])

            def turn_rows(src, t, c):
                for k in range(4):
                    last = turn(misc[:, 2 * t + c, k * P:(k + 1) * P], src[:, t, (4 * c + k) * P:(4 * c + k + 1) * P])
                last.then_inc(s_x_turned, 1)

            def turn_h(l, norm, t):
                for c in range(2):
                    pe.wait_ge(s_ln_norm, value("ln_norm", l, 2 * (TT * norm + t) + c + 1))
                    turn_rows(h, t, c)

            def x_ready(l, count):
                pe.wait_ge(s_x_ready, value("x_ready", l, count))

            def turn_qk(l):
                pe.wait_ge(s_rope_step, value("rope_step", l, 6))
                for i in range(QK_HEADS // 2):
                    if i == 4:
                        pe.wait_ge(s_qk_ready, value("qk_ready", l, 1))
                    for j in range(2):
                        for t in range(TT):
                            last = turn(misc[:, i % 4, (2 * j + t) * P:(2 * j + t + 1) * P], qk[:, t, 2 * i + j, :])
                    last.then_inc(s_qk_turned, 1)

            def scores(l, r):
                g, b = divmod(r, TT)
                if r == 0:
                    pe.wait_ge(s_qk_ready, value("qk_ready", l, 5))
                else:
                    pe.wait_ge(s_exp_done, value("exp_done", l, 5 * r))
                for i in range(GROUP):
                    last = nc.tensor.matmul(misc[:, i // 2, SEQ * (i % 2):SEQ * (i % 2 + 1)],
                                            qkT[:, GROUP * g + i, b * P:(b + 1) * P], qkT[:, HEADS + g, :],
                                            start=True, stop=True)
                last.then_inc(s_scores, 1)

            def turn_probs(l, r):
                pe.wait_ge(s_probs, value("probs", l, r + 1))
                if r:
                    pe.wait_ge(s_attn_ready, value("attn_ready", l, r))
                for kb in range(TT):
                    for i in range(GROUP):
                        last = turn(misc[:, 2 + kb, i * P:(i + 1) * P], soft[:, i, kb * P:(kb + 1) * P])
                last.then_inc(s_probs_turned, 1)

            def mix_values(l, r):
                pe.wait_ge(s_probs_back, value("probs_back", l, r + 1))
                for kb in range(TT):
                    last = nc.tensor.matmul(misc[:, 2, :], v[:, kb, r // TT, :], pT[:, kb, :, :],
                                            start=kb == 0, stop=kb == TT - 1)
                last.then_inc(s_mixed, 1)

            pe.sem_inc(s_products, BASE["products"])
            pe.sem_inc(s_p_turned, BASE["p_turned"])
            pe.wait_ge(s_const, 5)
            with pe.Fori(0, DEPTH) as l:
                x = (x_hi, x_lo)
                attn = (a_hi, a_lo)
                rnn = (r_hi, r_lo)
                turn_h(l, 0, 0)
                token_unit_by_tile(l, "q0", x, 0, after=lambda: q0_tile_1(l))
                feature_unit(l, "xr0")
                feature_half(l, "xr1", 0)
                gates_block(l, 0)
                feature_half(l, "xr1", 1)
                for i, name in enumerate(WITH_BLOCK[1:-1], 1):
                    token_half(l, name, 0, x)
                    if i >= 5:
                        mix_values(l, i - 5)
                    gates_block(l, i)
                    if name == "ga0":
                        turn_qk(l)
                    token_half(l, name, 1, x)
                    if i >= 4:
                        turn_probs(l, i - 4)
                    if i >= 3:
                        scores(l, i - 3)
                feature_half(l, "yr0", 0)
                mix_values(l, 2)
                gates_block(l, 7)
                feature_half(l, "yr0", 1)
                turn_probs(l, 3)
                feature_half(l, "yr1", 0)
                mix_values(l, 3)
                feature_half(l, "yr1", 1)
                pe.wait_ge(s_attn_ready, value("attn_ready", l, ROUNDS))
                token_unit(l, "pa0", attn)
                token_unit(l, "pa1", attn)
                pe.wait_ge(s_rnn_ready, value("rnn_ready", l, 1))
                token_half(l, "pr0", 0, rnn)
                pe.wait_ge(s_rnn_ready, value("rnn_ready", l, 2))
                token_half(l, "pr0", 1, rnn)
                token_half(l, "pr1", 0, rnn)
                for t in range(TT):
                    pe.wait_ge(s_merge, value("merge", l, t + 1))
                    turn_rows(ga, t, 0)
                token_half(l, "pr1", 1, rnn)
                pe.wait_ge(s_p, 16 * l + 16)
                for k in range(2):
                    for t in range(TT):
                        last = turn(misc[:, 1, (2 * k + t) * P:(2 * k + t + 1) * P], p_in[:, t, k * P:(k + 1) * P])
                last.then_inc(s_p_turned, 1)
                x_ready(l, 4 + 2)
                token_part(l, "wo0", 0, 0, x)
                pe.wait_ge(s_p_ready, value("p_ready", l, 1))
                for t in range(TT):
                    pe.wait_ge(s_merge, value("merge", l, 2 + t + 1))
                    turn_rows(ga, t, 1)
                token_part(l, "wo0", 0, 1, x).then_inc(s_products, 1)
                x_ready(l, 4 + 4)
                token_half(l, "wo0", 1, x)
                token_unit_by_tile(l, "wo1", x)
                ple_part(l, 0, 0)
                turn_h(l, 1, 0)
                ple_part(l, 0, 1)
                token_unit_by_tile(l, "pg0", x, 8, after=lambda: pg0_tile_1(l))
                for j in range(FF_GROUPS):
                    feature_unit(l, f"g{j}")
                    feature_unit(l, f"v{j}")
                    if j == FF_GROUPS - 1:
                        token_unit(l, "pg1", x)
                    if j:
                        down_unit(l, j - 1)
                last_down_unit(l)

        @block.scalar
        def _(act):
            def split_hi(l, n):
                slot = n % RAW_SLOTS
                act.wait_ge(s_raw[slot], l * LOADED_PER_LAYER[slot] + LOADED[n])
                used = AFTER_ITEM[n - W_SLOTS] if n >= W_SLOTS else AFTER_ITEM[n - W_SLOTS] - PER["products"]
                act.wait_ge(s_products, value("products", l, used))
                size = item_size(n)
                nc.scalar.copy(w_hi[:, n % W_SLOTS, 0:size], raw[:, slot, 0:size]).then_inc(s_hi_part, 1)

            split = [0]

            def split_to(l, name, part):
                while split[0] <= min(ITEM[name, part] + AHEAD, len(ITEMS) - 1):
                    split_hi(l, split[0])
                    split[0] += 1

            def x_parts(l, count, banks, scale):
                for i, (t, c) in enumerate(banks):
                    act.wait_ge(s_x_turned, value("x_turned", l, count + i + 1))
                    nc.scalar.activation(x_hi[:, 4 * c:4 * c + 4, t * P:(t + 1) * P], misc[:, 2 * t + c, :].rearrange("p (k t) -> p k t", k=4), ACT.Copy,
                                         scale=scale).then_inc(s_x_hi, 1)

            def out_of(l, name, part, dst, func, scale=1.0):
                key = (name, part)
                act.wait_ge(s_products, made(l, name, part))
                nc.scalar.activation(dst, bank_of(key), func, scale=scale).then_inc(s_emptied[RING[key][0]], 1)

            def conv_base(l, i):
                direction, b = divmod(i, RNN_BLOCKS)
                if i == 0:
                    act.wait_ge(s_small, 32 * l + 32)
                bank, before = RING[f"xr{b // 2}", b % 2]
                act.wait_ge(s_emptied[bank], l * RING_USES[bank] + before + 2)
                act.wait_ge(s_gated, value("gated", l, max(0, i - 1)))
                for j in range(2):
                    ft = 2 * b + j
                    last = nc.scalar.activation(xc[:, i % 2, j, :], xT[:, ft, :], ACT.Identity,
                                                bias=rnnp[:, direction, ft, 4:5], scale=rnnp[:, direction, ft, 0:1])
                last.then_inc(s_conv_base, 1)

            def conv_hi(l, i):
                direction, b = divmod(i, RNN_BLOCKS)
                act.wait_ge(s_conv_step, value("conv_step", l, 6 * (i + 1)))
                if direction:
                    act.wait_ge(s_products, made(l, "rg0", (b, 1)))
                nc.scalar.activation(r_hi[:, 2 * b:2 * b + 2, :], xc[:, i % 2], ACT.Copy,
                                     scale=1.0).then_inc(s_rin_hi, 1)

            def gate_curves(l, i):
                direction, b = divmod(i, RNN_BLOCKS)
                name = f"rg{direction}"
                if i == 0:
                    act.wait_ge(s_param_step, value("param_step", l, PER["param_step"]))
                act.wait_ge(s_m2_done, value("m2_done", l, max(0, i - 1)))
                act.wait_ge(s_gated, value("gated", l, max(0, i - 1)))
                for g, dst in ((0, ta), (1, tx)):
                    key = (name, (b, g))
                    act.wait_ge(s_products, made(l, name, (b, g)))
                    for d in range(2):
                        last = nc.scalar.activation(dst[:, i % 2, d, :], bank_of(key)[:, SEQ * d:SEQ * (d + 1)],
                                                    ACT.Tanh, bias=rnnd[:, g, direction, 2 * b + d:2 * b + d + 1],
                                                    scale=0.5)
                    last.then_inc(s_emptied[RING[key][0]], 1)
                if b % 2 == 0:
                    act.wait_ge(s_scanned, value("scanned", l, i // 2))
                act.wait_ge(s_emptied[RING[(name, (b, 0))][0]], read_out(l, (name, (b, 0))))
                at = 2 * (b % 2)
                for d in range(2):
                    ft = 2 * b + d
                    last = nc.scalar.activation(decay_a[:, at + d, :], ta[:, i % 2, d, :], ACT.Exp,
                                                bias=coef[:, 1, direction, ft:ft + 1],
                                                scale=coef[:, 1, direction, ft:ft + 1])
                last.then_inc(s_decay, 1)
                for d in range(2):
                    ft = 2 * b + d
                    last = nc.scalar.activation(root_m[:, at + d, :], ta[:, i % 2, d, :], ACT.Tanh,
                                                bias=coef[:, 0, direction, ft:ft + 1],
                                                scale=coef[:, 0, direction, ft:ft + 1])
                last.then_inc(s_decay, 1)
                act.wait_ge(s_decay, value("decay", l, 2 * i + 2))
                nc.scalar.activation(ta[:, i % 2], decay_a[:, at:at + 2, :], ACT.Square).then_inc(s_pair_ready, 1)

            def root(l, g):
                act.wait_ge(s_m2_done, value("m2_done", l, 2 * g + 2))
                nc.scalar.activation(root_m[:, :, :], root_m[:, :, :], ACT.Sqrt, scale=0.25).then_inc(s_root, 1)

            def rnn_out(l, c):
                act.wait_ge(s_rnn_step, value("rnn_step", l, 2 * c + 2))
                nc.scalar.activation(r_hi[:, 4 * c:4 * c + 4, :], hf[:, 4 * c:4 * c + 4, :], ACT.Copy,
                                     scale=1.0).then_inc(s_rnn_hi, 1)

            def exponentials(l, r):
                act.wait_ge(s_soft_step, value("soft_step", l, 6 * r + 4))
                for i in range(GROUP):
                    nc.scalar.activation(soft[:, i, :], misc[:, i // 2, SEQ * (i % 2):SEQ * (i % 2 + 1)], ACT.Exp,
                                         bias=sm[:, 1, i:i + 1], scale=SCALE,
                                         accum_out=sm[:, 3, i:i + 1]).then_inc(s_exp_done, 1)
                nc.scalar.activation(sm[:, 4, :], sm[:, 2, :], ACT.Exp).then_inc(s_exp_done, 1)

            def probs_back(l, r):
                act.wait_ge(s_probs_turned, value("probs_turned", l, r + 1))
                nc.scalar.copy(pT[:, :, :, :].rearrange("p a g t -> p (a g t)"),
                               misc[:, 2:4, :].rearrange("p a n -> p (a n)")).then_inc(s_probs_back, 1)

            def attn_out(l, r):
                g, b = divmod(r, TT)
                act.wait_ge(s_mixed, value("mixed", l, r + 1))
                nc.scalar.activation(a_hi[:, GROUP * g:GROUP * (g + 1), b * P:(b + 1) * P], misc[:, 2, :].rearrange("p (i t) -> p i t", i=GROUP), ACT.Copy,
                                     scale=1.0).then_inc(s_attn_hi, 1)

            def gate_base(l, j, hh):
                if j == 0 and hh == 0:
                    act.wait_ge(s_ffnp, 16 * l + 16)
                act.wait_ge(s_products, made(l, f"g{j}", hh))
                act.wait_ge(s_f_ready, value("f_ready", l, max(0, 2 * (j - 2) + hh + 1)))
                for d in range(2):
                    ft = 4 * j + 2 * hh + d
                    last = nc.scalar.activation(tmp[:, hh + 2 * (j % 2), d, :],
                                                bank_of((f"g{j}", hh))[:, SEQ * d:SEQ * (d + 1)], ACT.Identity,
                                                bias=ffnp[:, ft, 3:4], scale=ffnp[:, ft, 1:2])
                last.then_inc(s_gate_base, 1)

            def gelu(l, j, hh):
                act.wait_ge(s_emptied[RING[(f"g{j}", hh)][0]], read_out(l, (f"g{j}", hh)))
                c = tmp[:, hh + 2 * (j % 2)]
                nc.scalar.activation(c, c, ACT.Gelu_apprx_tanh).then_inc(s_gelu, 1)

            def hidden_hi(l, j, hh):
                act.wait_ge(s_emptied[RING[(f"v{j}", hh)][0]], read_out(l, (f"v{j}", hh)))
                if j >= 2 and hh == 0:
                    act.wait_ge(s_products, value("products", l, PRODUCT[f"d{j - 2}", 1]))
                at = 4 * (j % 2) + 2 * hh
                nc.scalar.activation(a_hi[:, at:at + 2, :], tmp[:, hh + 2 * (j % 2)], ACT.Copy,
                                     scale=1.0).then_inc(s_f_hi, 1)

            def qk_copies(l):
                for i in range(5):
                    act.wait_ge(s_qk_turned, value("qk_turned", l, i + 1))
                    nc.scalar.copy(qkT[:, 2 * i:2 * i + 2, :].rearrange("p k s -> p (k s)"),
                                   misc[:, i % 4, :]).then_inc(s_qk_ready, 1)

            def unit_out(l, name):
                for t in range(TT):
                    if name in ("q0", "q1"):
                        i = int(name[1])
                        out_of(l, name, t, qk[:, t, 4 * i:4 * i + 4, :].rearrange("p h d -> p (h d)"), ACT.Copy)
                    elif name == "kv":
                        act.wait_ge(s_products, made(l, "kv", t))
                        nc.scalar.copy(qk[:, t, HEADS:QK_HEADS, :].rearrange("p h d -> p (h d)"),
                                       bank_of(("kv", t))[:, 0:KV_WIDTH])
                        nc.scalar.copy(v[:, t].rearrange("p h d -> p (h d)"),
                                       bank_of(("kv", t))[:, KV_WIDTH:2 * KV_WIDTH]).then_inc(
                            s_emptied[RING["kv", t][0]], 1)
                    else:
                        dst, c = (ga if name[:2] == "ga" else gr), int(name[2])
                        out_of(l, name, t, dst[:, t, 512 * c:512 * c + 512], ACT.Tanh, 0.5)

            def xr_out(l, unit, hh):
                at = 4 * unit + 2 * hh
                out_of(l, f"xr{unit}", hh, xT[:, at:at + 2, :].rearrange("p k s -> p (k s)"), ACT.Copy)

            def yr_out(l, unit, hh):
                at = 4 * unit + 2 * hh
                out_of(l, f"yr{unit}", hh, yg[:, at:at + 2, :].rearrange("p k s -> p (k s)"), ACT.Gelu_apprx_tanh)

            def pg_out(l, c, t):
                out_of(l, f"pg{c}", t, gr[:, t, 512 * c:512 * c + 512], ACT.Tanh, 0.5)

            act.wait_ge(s_h[0], 16)
            act.dma_start(h[:, 1, :], a["x"][0, P:SEQ, :]).then_inc(s_h[1], 16)
            act.dma_start(rope[:], a["rope"]).then_inc(s_rope, 16)
            with act.Fori(0, DEPTH) as l:
                split_hi(l, 0)
                x_parts(l, 0, [(0, 0), (0, 1)], 1.0)
                split_hi(l, 1)
                split[0] = 2
                split_to(l, "q0", 0)
                x_parts(l, 2, [(1, 0), (1, 1)], 1.0)
                split_to(l, "q0", 1)
                unit_out(l, "q0")
                act.wait_ge(s_param_step, value("param_step", l, 1))
                nc.scalar.activation(lam_t[:, 1], lam_t[:, 0], ACT.Exp).then_inc(s_param_exp, 1)
                split_to(l, "xr0", 0)
                xr_out(l, 0, 0)
                conv_base(l, 0)
                split_to(l, "xr0", 1)
                xr_out(l, 0, 1)
                conv_hi(l, 0)
                conv_base(l, 1)
                split_to(l, "xr1", 0)
                xr_out(l, 1, 0)
                conv_hi(l, 1)
                split_to(l, "rg0", 0)
                gate_curves(l, 0)
                split_to(l, "xr1", 1)
                xr_out(l, 1, 1)
                conv_base(l, 2)
                for i, name in enumerate(WITH_BLOCK[1:], 1):
                    if i >= 5:
                        probs_back(l, i - 5)
                    split_to(l, name, 0)
                    if i >= 4:
                        exponentials(l, i - 4)
                    if i + 1 < 2 * RNN_BLOCKS:
                        conv_hi(l, i + 1)
                    split_to(l, f"rg{i // RNN_BLOCKS}", i % RNN_BLOCKS)
                    if i >= 5:
                        attn_out(l, i - 5)
                    gate_curves(l, i)
                    if name == "ga0":
                        qk_copies(l)
                    split_to(l, name, 1)
                    if i + 2 < 2 * RNN_BLOCKS:
                        conv_base(l, i + 2)
                    if i % 2 == 1:
                        root(l, i // 2)
                    if name == "gr0":
                        act.wait_ge(s_conv_step, value("conv_step", l, PER["conv_step"]))
                    if name != "yr0":
                        unit_out(l, name)
                yr_out(l, 0, 0)
                yr_out(l, 0, 1)
                probs_back(l, 3)
                split_to(l, "yr1", 0)
                yr_out(l, 1, 0)
                attn_out(l, 3)
                split_to(l, "yr1", 1)
                yr_out(l, 1, 1)
                rnn_out(l, 0)
                split_to(l, "pa0", 0)
                rnn_out(l, 1)
                split_to(l, "pr1", 0)
                x_parts(l, 4, [(0, 0), (1, 0)], 0.5)
                split_to(l, "pr1", 1)
                act.wait_ge(s_p_turned, value("p_turned", l, 1))
                nc.scalar.activation(r_hi[:, 0:2, :].rearrange("p k s -> p (k s)"), misc[:, 1, :], ACT.Copy,
                                     scale=1.0).then_inc(s_p_hi, 1)
                split_to(l, "wo0", 0)
                x_parts(l, 6, [(0, 1), (1, 1)], 0.5)
                split_to(l, "wo1", 1)
                x_parts(l, 8, [(0, 0), (0, 1)], 1.0)
                split_to(l, "ple", 0)
                for t in range(TT):
                    out_of(l, "ple", (0, t), ga[:, t, 0:512], ACT.Copy, 0.5)
                split_to(l, "pg0", 0)
                pg_out(l, 0, 0)
                x_parts(l, 10, [(1, 0), (1, 1)], 1.0)
                for t in range(TT):
                    out_of(l, "ple", (1, t), ga[:, t, 512:1024], ACT.Copy, 0.5)
                split_to(l, "pg0", 1)
                pg_out(l, 0, 1)
                for j in range(FF_GROUPS):
                    for hh in range(2):
                        split_to(l, f"g{j}", hh)
                        gate_base(l, j, hh)
                    for hh in range(2):
                        split_to(l, f"v{j}", hh)
                        gelu(l, j, hh)
                        hidden_hi(l, j, hh)
                    if j == FF_GROUPS - 1:
                        split_to(l, "pg1", 1)
                        for t in range(TT):
                            pg_out(l, 1, t)
                    if j:
                        split_to(l, f"d{j - 1}", 1)

        @block.vector
        def _(dve):
            def split_lo(l, n):
                dve.wait_ge(s_hi_part, value("hi_part", l, n + 1))
                size = item_size(n)
                hi = w_hi[:, n % W_SLOTS, 0:size].bitcast(F32)
                nc.vector.tensor_tensor(w_lo[:, n % W_SLOTS, 0:size], raw[:, n % RAW_SLOTS, 0:size], hi,
                                        ALU.subtract).then_inc(s_split, 1)

            split = [0]

            def split_to(l, name, part):
                while split[0] <= min(ITEM[name, part] + AHEAD, len(ITEMS) - 1):
                    split_lo(l, split[0])
                    split[0] += 1

            def norm_step(l, n, t, k):
                dve.wait_ge(s_ln_step, value("ln_step", l, STATS_DONE[n][t] + k))

            def norm_stats(l, n, t, c):
                nc.vector.bn_stats(st[:, t, c, :], h[:, t, 512 * c:512 * c + 512]).then_inc(s_ln_step, 1)

            def norm_rest(l, n, t):
                norm_step(l, n, t, 0)
                nc.vector.memset(mv[:, t, 6:7], 0.0)
                nc.vector.bn_aggr(mv[:, t, 0:2], st[:, t]).then_inc(s_ln_step, 1)
                norm_step(l, n, t, 1)
                mean, var = mv[:, t, 0:1], mv[:, t, 1:2]
                var_eps, nhalf, y, u = (mv[:, t, i:i + 1] for i in range(2, 6))
                nc.vector.tensor_scalar(var_eps, var, LN_EPS, None, ALU.add).then_inc(s_ln_step, 1)
                nc.vector.tensor_scalar(nhalf, var, LN_EPS, -0.5, ALU.add, ALU.mult).then_inc(s_ln_step, 1)
                norm_step(l, n, t, 2)
                nc.vector.tensor_scalar(y.bitcast(I32), var_eps.bitcast(I32), -0.5, RSQRT_MAGIC,
                                        ALU.mult, ALU.add).then_inc(s_ln_step, 1)
                for i in range(3):
                    norm_step(l, n, t, 4 + 2 * i)
                    nc.vector.scalar_tensor_tensor(out=u, in0=y, scalar=y, in1=nhalf, op0=ALU.mult,
                                                   op1=ALU.mult).then_inc(s_ln_step, 1)
                    norm_step(l, n, t, 5 + 2 * i)
                    nc.vector.scalar_tensor_tensor(out=y, in0=u, scalar=1.5, in1=y, op0=ALU.add,
                                                   op1=ALU.mult).then_inc(s_ln_step, 1)
                dve.wait_ge(s_lnp, 32 * l + 16 * n + 16)
                for c in range(2):
                    at = slice(512 * c, 512 * c + 512)
                    nc.vector.scalar_tensor_tensor(out=h[:, t, at], in0=h[:, t, at], scalar=mean, in1=lnp[:, 0, at],
                                                   op0=ALU.subtract, op1=ALU.mult).then_inc(s_ln_step, 1)
                for c in range(2):
                    at = slice(512 * c, 512 * c + 512)
                    norm_step(l, n, t, 11 + c)
                    nc.vector.scalar_tensor_tensor(out=h[:, t, at], in0=h[:, t, at], scalar=y, in1=lnp[:, 1, at],
                                                   op0=ALU.mult, op1=ALU.add).then_inc(s_ln_norm, 1)

            def add_ffn(l, t):
                dve.wait_ge(s_ple_step, value("ple_step", l, 0))
                dve.wait_ge(s_h[t], 16)
                for c in range(2):
                    dve.wait_ge(s_products, value("products", l, PRODUCT[f"d{LAST}", (t, c)] - PER["products"]))
                    at = h[:, t, 512 * c:512 * c + 512]
                    nc.vector.tensor_tensor(at, at, misc[:, 2 * t + c, :], ALU.add).then_inc(s_added, 1)
                    dve.wait_ge(s_added, value("added", l, 2 * t + c + 1))
                    norm_stats(l, 0, t, c)

            def x_parts(l, count, banks, scale):
                for i, (t, c) in enumerate(banks):
                    dve.wait_ge(s_x_hi, value("x_hi", l, count + i + 1))
                    nc.vector.scalar_tensor_tensor(
                        out=x_lo[:, 4 * c:4 * c + 4, t * P:(t + 1) * P],
                        in0=misc[:, 2 * t + c, :].rearrange("p (k t) -> p k t", k=4), scalar=scale,
                        in1=x_hi[:, 4 * c:4 * c + 4, t * P:(t + 1) * P].bitcast(F32),
                        op0=ALU.mult, op1=ALU.subtract).then_inc(s_x_ready, 1)

            def params(l):
                dve.wait_ge(s_small, 32 * l + 32)
                lam = rnnp[:, :, :, 7]
                neg_abs, e, z, z2, poly, low = (lam_t[:, i] for i in range(6))
                nc.vector.scalar_tensor_tensor(out=neg_abs, in0=lam, scalar=-1.0, in1=lam, op0=ALU.mult,
                                               op1=ALU.min).then_inc(s_param_step, 1)
                nc.vector.tensor_scalar(rnnd[:, 0], rnnp[:, :, :, 5], 0.5, None, ALU.mult)
                nc.vector.tensor_scalar(rnnd[:, 1], rnnp[:, :, :, 6], 0.5, None, ALU.mult)
                nc.vector.tensor_scalar(nsink[:], sink[:], -1.0, None, ALU.mult)
                nc.vector.tensor_scalar(low, lam, 0.0, 4.0, ALU.min, ALU.mult).then_inc(s_param_step, 1)
                dve.wait_ge(s_param_exp, value("param_exp", l, 1))
                nc.vector.tensor_scalar(z2, e, 2.0, None, ALU.add).then_inc(s_param_step, 1)
                dve.wait_ge(s_param_step, value("param_step", l, 3))
                nc.vector.reciprocal(z2, z2).then_inc(s_param_step, 1)
                dve.wait_ge(s_param_step, value("param_step", l, 4))
                nc.vector.tensor_tensor(z, e, z2, ALU.mult).then_inc(s_param_step, 1)
                dve.wait_ge(s_param_step, value("param_step", l, 5))
                nc.vector.tensor_tensor(z2, z, z, ALU.mult).then_inc(s_param_step, 1)
                dve.wait_ge(s_param_step, value("param_step", l, 6))
                nc.vector.tensor_scalar(poly, z2, 1.0 / 15.0, None, ALU.mult).then_inc(s_param_step, 1)
                for i, k in enumerate((13, 11, 9, 7, 5, 3)):
                    dve.wait_ge(s_param_step, value("param_step", l, 7 + i))
                    nc.vector.scalar_tensor_tensor(out=poly, in0=poly, scalar=1.0 / k, in1=z2, op0=ALU.add,
                                                   op1=ALU.mult).then_inc(s_param_step, 1)
                dve.wait_ge(s_param_step, value("param_step", l, 13))
                nc.vector.scalar_tensor_tensor(out=poly, in0=poly, scalar=1.0, in1=z, op0=ALU.add,
                                               op1=ALU.mult).then_inc(s_param_step, 1)
                dve.wait_ge(s_param_step, value("param_step", l, 14))
                nc.vector.scalar_tensor_tensor(out=coef[:, 1], in0=poly, scalar=-8.0, in1=low, op0=ALU.mult,
                                               op1=ALU.add).then_inc(s_param_step, 1)
                dve.wait_ge(s_param_step, value("param_step", l, 15))
                nc.vector.tensor_scalar(coef[:, 0], coef[:, 1], -1.0, None, ALU.mult).then_inc(s_param_step, 1)

            def rotate(l):
                dve.wait_ge(s_rope, 16)
                all_emptied(dve, l, [(name, t) for name in ("q0", "q1", "kv") for t in range(TT)])
                x1, x2 = qk[:, :, :, 0:ROPE_HALF], qk[:, :, :, ROPE_HALF:ROPE_DIM]
                cos, sin = (rope[:, i].unsqueeze(2).broadcast_to((P, TT, QK_HEADS, ROPE_HALF)) for i in range(2))
                for i, (x, c) in enumerate(((x1, cos), (x2, sin), (x2, cos), (x1, sin))):
                    nc.vector.tensor_tensor(rope_t[i // 2][:, i % 2], x, c, ALU.mult).then_inc(s_rope_step, 1)
                dve.wait_ge(s_rope_step, value("rope_step", l, 4))
                nc.vector.tensor_tensor(x1, rope_t[0][:, 0], rope_t[0][:, 1], ALU.subtract).then_inc(s_rope_step, 1)
                nc.vector.tensor_tensor(x2, rope_t[1][:, 0], rope_t[1][:, 1], ALU.add).then_inc(s_rope_step, 1)

            def softmax_max(l, r):
                g, b = divmod(r, TT)
                dve.wait_ge(s_scores, value("scores", l, r + 1))
                logits = misc[:, 0:2, :].rearrange("p a (i s) -> p (a i) s", i=2)
                other = logits[:, :, (1 - b) * P:(2 - b) * P]
                mask = masks[:, b, :].unsqueeze(1).broadcast_to((P, GROUP, P))
                nc.vector.tensor_tensor(other, other, mask, ALU.add).then_inc(s_soft_step, 1)
                dve.wait_ge(s_soft_step, value("soft_step", l, 6 * r + 1))
                nc.vector.tensor_reduce(sm[:, 0, :], logits, AX_X, ALU.max).then_inc(s_soft_step, 1)
                dve.wait_ge(s_soft_step, value("soft_step", l, 6 * r + 2))
                if r:
                    dve.wait_ge(s_exp_done, value("exp_done", l, 5 * r))
                heads = slice(GROUP * g, GROUP * (g + 1))
                nc.vector.scalar_tensor_tensor(out=sm[:, 1, :], in0=sm[:, 0, :], scalar=-SCALE, in1=nsink[:, heads],
                                               op0=ALU.mult, op1=ALU.min).then_inc(s_soft_step, 1)
                dve.wait_ge(s_soft_step, value("soft_step", l, 6 * r + 3))
                nc.vector.tensor_tensor(sm[:, 2, :], sm[:, 1, :], sink[:, heads], ALU.add).then_inc(s_soft_step, 1)

            def softmax_norm(l, r):
                dve.wait_ge(s_exp_done, value("exp_done", l, 5 * r + 5))
                nc.vector.tensor_tensor(sm[:, 5, :], sm[:, 3, :], sm[:, 4, :], ALU.add).then_inc(s_soft_step, 1)
                dve.wait_ge(s_soft_step, value("soft_step", l, 6 * r + 5))
                nc.vector.reciprocal(sm[:, 5, :], sm[:, 5, :]).then_inc(s_soft_step, 1)
                dve.wait_ge(s_soft_step, value("soft_step", l, 6 * r + 6))
                for i in range(GROUP):
                    last = nc.vector.tensor_scalar(soft[:, i, :], soft[:, i, :], sm[:, 5, i:i + 1], None, ALU.mult)
                last.then_inc(s_probs, 1)

            def attn_out(l, r):
                g, b = divmod(r, TT)
                at = (slice(None), slice(GROUP * g, GROUP * (g + 1)), slice(b * P, (b + 1) * P))
                dve.wait_ge(s_attn_hi, value("attn_hi", l, r + 1))
                nc.vector.tensor_tensor(a_lo[at], misc[:, 2, :].rearrange("p (i t) -> p i t", i=GROUP), a_hi[at].bitcast(F32),
                                        ALU.subtract).then_inc(s_attn_ready, 1)

            def conv(l, i):
                direction, b = divmod(i, RNN_BLOCKS)
                dve.wait_ge(s_conv_base, value("conv_base", l, i + 1))
                for k in range(1, CONV_W):
                    for j in range(2):
                        ft = 2 * b + j
                        if k > 1:
                            dve.wait_ge(s_conv_step, value("conv_step", l, 6 * i + 2 * (k - 2) + j + 1))
                        to, frm = (slice(k, SEQ), slice(0, SEQ - k)) if direction == 0 else \
                            (slice(0, SEQ - k), slice(k, SEQ))
                        nc.vector.scalar_tensor_tensor(
                            out=xc[:, i % 2, j, to], in0=xT[:, ft, frm], scalar=rnnp[:, direction, ft, k:k + 1],
                            in1=xc[:, i % 2, j, to], op0=ALU.mult, op1=ALU.add).then_inc(s_conv_step, 1)

            def conv_lo(l, i):
                b = i % RNN_BLOCKS
                dve.wait_ge(s_rin_hi, value("rin_hi", l, i + 1))
                nc.vector.tensor_tensor(r_lo[:, 2 * b:2 * b + 2, :], xc[:, i % 2], r_hi[:, 2 * b:2 * b + 2, :].bitcast(F32),
                                        ALU.subtract).then_inc(s_rin_ready, 1)

            def gate_input(l, i):
                direction, b = divmod(i, RNN_BLOCKS)
                state = hb if direction else hf
                dve.wait_ge(s_emptied[RING[(f"rg{direction}", (b, 1))][0]], read_out(l, (f"rg{direction}", (b, 1))))
                nc.vector.scalar_tensor_tensor(out=state[:, 2 * b:2 * b + 2, :], in0=tx[:, i % 2], scalar=1.0,
                                               in1=xc[:, i % 2], op0=ALU.add, op1=ALU.mult).then_inc(s_gated, 1)
                at = 2 * (b % 2)
                dve.wait_ge(s_pair_ready, value("pair_ready", l, i + 1))
                nc.vector.scalar_tensor_tensor(out=root_m[:, at:at + 2, :], in0=ta[:, i % 2], scalar=1.0,
                                               in1=root_m[:, at:at + 2, :], op0=ALU.add,
                                               op1=ALU.mult).then_inc(s_m2_done, 1)

            def scan(l, g):
                direction, c = divmod(g, 2)
                state = (hb if direction else hf)[:, 4 * c:4 * c + 4, :]
                first = SEQ - 1 if direction else 0
                dve.wait_ge(s_root, value("root", l, g + 1))
                nc.vector.memset(root_m[:, :, first:first + 1], 0.5).then_inc(s_rg_step, 1)
                nc.vector.memset(decay_a[:, :, first:first + 1], 0.0).then_inc(s_rg_step, 1)
                dve.wait_ge(s_rg_step, value("rg_step", l, 3 * g + 2))
                nc.vector.tensor_tensor(state, state, root_m[:, :, :], ALU.mult).then_inc(s_rg_step, 1)
                dve.wait_ge(s_rg_step, value("rg_step", l, 3 * g + 3))
                flat = state.rearrange("p k s -> p (k s)")
                decays = decay_a[:, :, :].rearrange("p k s -> p (k s)")
                if direction:
                    flat, decays = flat[:, ::-1], decays[:, ::-1]
                nc.vector.tensor_tensor_scan(flat, decays, flat, 0.0, ALU.mult, ALU.add).then_inc(s_scanned, 1)

            def rnn_out(l, c):
                at = slice(4 * c, 4 * c + 4)
                dve.wait_ge(s_scanned, value("scanned", l, 3 + c))
                nc.vector.tensor_tensor(hf[:, at, :], hf[:, at, :], hb[:, at, :], ALU.add).then_inc(s_rnn_step, 1)
                if c == 0:
                    all_emptied(dve, l, [(name, hh) for name in ("yr0", "yr1") for hh in range(2)])
                dve.wait_ge(s_rnn_step, value("rnn_step", l, 2 * c + 1))
                nc.vector.tensor_tensor(hf[:, at, :], hf[:, at, :], yg[:, at, :], ALU.mult).then_inc(s_rnn_step, 1)

            def rnn_lo(l, c):
                at = slice(4 * c, 4 * c + 4)
                dve.wait_ge(s_rnn_hi, value("rnn_hi", l, c + 1))
                nc.vector.tensor_tensor(r_lo[:, at, :], hf[:, at, :], r_hi[:, at, :].bitcast(F32),
                                        ALU.subtract).then_inc(s_rnn_ready, 1)

            def gated_projection(l, name, gate, c, t):
                key = (name, t)
                dve.wait_ge(s_products, made(l, name, t))
                at = gate[:, t, 512 * c:512 * c + 512]
                nc.vector.scalar_tensor_tensor(out=at, in0=at, scalar=1.0, in1=bank_of(key), op0=ALU.add,
                                               op1=ALU.mult).then_inc(s_emptied[RING[key][0]], 1)

            def outer_taps(l, j, hh):
                dve.wait_ge(s_gate_base, value("gate_base", l, 2 * j + hh + 1))
                c = tmp[:, hh + 2 * (j % 2)]
                bank = bank_of((f"g{j}", hh))
                for d in range(2):
                    ft = 4 * j + 2 * hh + d
                    nc.vector.scalar_tensor_tensor(
                        out=c[:, d, 1:SEQ], in0=bank[:, SEQ * d:SEQ * (d + 1) - 1], scalar=ffnp[:, ft, 0:1],
                        in1=c[:, d, 1:SEQ], op0=ALU.mult, op1=ALU.add).then_inc(s_tap_step, 1)
                for d in range(2):
                    ft = 4 * j + 2 * hh + d
                    dve.wait_ge(s_tap_step, value("tap_step", l, 4 * j + 2 * hh + d + 1))
                    last = nc.vector.scalar_tensor_tensor(
                        out=c[:, d, 0:SEQ - 1], in0=bank[:, SEQ * d + 1:SEQ * (d + 1)], scalar=ffnp[:, ft, 2:3],
                        in1=c[:, d, 0:SEQ - 1], op0=ALU.mult, op1=ALU.add)
                last.then_inc(s_emptied[RING[f"g{j}", hh][0]], 1)

            def hidden(l, j, hh):
                key = (f"v{j}", hh)
                dve.wait_ge(s_products, made(l, *key))
                dve.wait_ge(s_gelu, value("gelu", l, 2 * j + hh + 1))
                c = tmp[:, hh + 2 * (j % 2)]
                nc.vector.tensor_tensor(c, c, bank_of(key).rearrange("p (d s) -> p d s", d=2), ALU.mult).then_inc(
                    s_emptied[RING[key][0]], 1)

            def hidden_lo(l, j, hh):
                dve.wait_ge(s_f_hi, value("f_hi", l, 2 * j + hh + 1))
                at = slice(4 * (j % 2) + 2 * hh, 4 * (j % 2) + 2 * hh + 2)
                nc.vector.tensor_tensor(a_lo[:, at, :], tmp[:, hh + 2 * (j % 2)], a_hi[:, at, :].bitcast(F32),
                                        ALU.subtract).then_inc(s_f_ready, 1)

            def out_proj(l, c, t):
                key = (f"wo{c}", t)
                dve.wait_ge(s_products, made(l, *key))
                at = h[:, t, 512 * c:512 * c + 512]
                nc.vector.scalar_tensor_tensor(out=at, in0=at, scalar=ALPHA, in1=bank_of(key), op0=ALU.mult,
                                               op1=ALU.add).then_inc(s_emptied[RING[key][0]], 1)

            for begin, count in ((s_split, BASE["split"]), (s_ln_norm, 1), (s_rnn_ready, 1), (s_f_ready, 1),
                                 (s_gated, 1), (s_m2_done, 1), (s_scanned, 1), *((s, 1) for s in s_emptied)):
                dve.sem_inc(begin, count)
            nc.vector.memset(misc[:], 0.0).then_inc(s_ple_step, 1)
            with dve.Fori(0, DEPTH) as l:
                add_ffn(l, 0)
                norm_rest(l, 0, 0)
                split_lo(l, 0)
                x_parts(l, 0, [(0, 0), (0, 1)], 1.0)
                split_lo(l, 1)
                add_ffn(l, 1)
                norm_rest(l, 0, 1)
                x_parts(l, 2, [(1, 0), (1, 1)], 1.0)
                split[0] = 2
                split_to(l, "q0", 0)
                split_to(l, "q0", 1)
                params(l)
                split_to(l, "xr0", 0)
                conv(l, 0)
                split_to(l, "xr0", 1)
                conv_lo(l, 0)
                conv(l, 1)
                split_to(l, "xr1", 0)
                conv_lo(l, 1)
                split_to(l, "rg0", 0)
                gate_input(l, 0)
                split_to(l, "xr1", 1)
                conv(l, 2)
                for i, name in enumerate(WITH_BLOCK[1:], 1):
                    if name == "ga0":
                        rotate(l)
                    if i >= 5:
                        softmax_max(l, i - 4)
                    split_to(l, name, 0)
                    if i + 1 < 2 * RNN_BLOCKS:
                        conv_lo(l, i + 1)
                    split_to(l, f"rg{i // RNN_BLOCKS}", i % RNN_BLOCKS)
                    if i >= 4:
                        softmax_norm(l, i - 4)
                    if i >= 5:
                        attn_out(l, i - 5)
                    gate_input(l, i)
                    split_to(l, name, 1)
                    if i + 2 < 2 * RNN_BLOCKS:
                        conv(l, i + 2)
                    if i == 3:
                        softmax_max(l, 0)
                    if i % 2 == 1:
                        scan(l, i // 2)
                split_to(l, "yr1", 0)
                attn_out(l, 3)
                rnn_out(l, 0)
                split_to(l, "yr1", 1)
                rnn_lo(l, 0)
                rnn_out(l, 1)
                split_to(l, "pa0", 0)
                rnn_lo(l, 1)
                split_to(l, "pa0", 1)
                for c in range(2):
                    split_to(l, f"pa{c}", 1)
                    for t in range(TT):
                        if c == 0 and t == 0:
                            all_emptied(dve, l, [(name, i) for name in ("ga0", "ga1") for i in range(TT)])
                        gated_projection(l, f"pa{c}", ga, c, t)
                for c in range(2):
                    split_to(l, f"pr{c}", 1)
                    for t in range(TT):
                        if c == 0 and t == 0:
                            all_emptied(dve, l, [(name, i) for name in ("gr0", "gr1") for i in range(TT)])
                        gated_projection(l, f"pr{c}", gr, c, t)
                    all_emptied(dve, l, [(f"pr{c}", t) for t in range(TT)])
                    for t in range(TT):
                        at = (slice(None), t, slice(512 * c, 512 * c + 512))
                        nc.vector.tensor_tensor(ga[at], ga[at], gr[at], ALU.add).then_inc(s_merge, 1)
                    if c == 0:
                        split_to(l, "pr1", 0)
                        x_parts(l, 4, [(0, 0), (1, 0)], 0.5)
                dve.wait_ge(s_p_hi, value("p_hi", l, 1))
                nc.vector.tensor_tensor(r_lo[:, 0:2, :].rearrange("p k s -> p (k s)"), misc[:, 1, :],
                                        r_hi[:, 0:2, :].rearrange("p k s -> p (k s)").bitcast(F32),
                                        ALU.subtract).then_inc(s_p_ready, 1)
                split_to(l, "wo0", 0)
                x_parts(l, 6, [(0, 1), (1, 1)], 0.5)
                split_to(l, "wo0", 1)
                for t in range(TT):
                    out_proj(l, 0, t)
                    all_emptied(dve, l, [("wo0", t)])
                    norm_stats(l, 1, t, 0)
                split_to(l, "wo1", 0)
                out_proj(l, 1, 0)
                all_emptied(dve, l, [("wo1", 0)])
                norm_stats(l, 1, 0, 1)
                norm_rest(l, 1, 0)
                split_to(l, "wo1", 1)
                x_parts(l, 8, [(0, 0), (0, 1)], 1.0)
                out_proj(l, 1, 1)
                all_emptied(dve, l, [("wo1", 1)])
                norm_stats(l, 1, 1, 1)
                split_to(l, "ple", 0)
                norm_rest(l, 1, 1)
                split_to(l, "pg0", 0)
                x_parts(l, 10, [(1, 0), (1, 1)], 1.0)
                split_to(l, "pg0", 1)
                for j in range(FF_GROUPS):
                    for hh in range(2):
                        split_to(l, f"g{j}", hh)
                        outer_taps(l, j, hh)
                    for hh in range(2):
                        split_to(l, f"v{j}", hh)
                        hidden(l, j, hh)
                        hidden_lo(l, j, hh)
                    if j == FF_GROUPS - 1:
                        split_to(l, "pg1", 1)
                    if j:
                        split_to(l, f"d{j - 1}", 1)
                all_emptied(dve, l, [(f"pg{c}", t) for c in range(2) for t in range(TT)]
                            + [("ple", (c, t)) for c in range(2) for t in range(TT)])
                flat = ga[:, :, :].rearrange("p t n -> p (t n)")
                h_flat = h[:, :, :].rearrange("p t n -> p (t n)")
                nc.vector.scalar_tensor_tensor(out=flat, in0=gr.rearrange("p t n -> p (t n)"), scalar=1.0, in1=flat,
                                               op0=ALU.add, op1=ALU.mult).then_inc(s_ple_step, 1)
                dve.wait_ge(s_ple_step, value("ple_step", l, 1))
                nc.vector.scalar_tensor_tensor(out=h_flat, in0=h_flat, scalar=ALPHA, in1=flat, op0=ALU.mult,
                                               op1=ALU.add).then_inc(s_ple_step, 1)
            for t in range(TT):
                add_ffn(DEPTH, t)
                norm_rest(DEPTH, 0, t)


def rope_tables():
    pos = np.arange(SEQ, dtype=np.float32)
    inv = np.float32(ROPE_THETA) ** (-np.arange(0, ROPE_DIM, 2, dtype=np.float32) / np.float32(ROPE_DIM))
    ang = pos[:, None] * inv[None, :].astype(np.float32)
    both = np.stack([np.cos(ang), np.sin(ang)]).astype(np.float32)
    return np.ascontiguousarray(both.reshape(2, TT, P, ROPE_HALF).transpose(2, 0, 1, 3))


_AS_THEY_COME = ["x", "p", "w_in", "attn_sink", "rg_w_a", "rg_w_x", "w_proj_attn", "w_proj_rnn", "w_out",
                 "w_up", "w_down", "w_ple", "w_ple_gate"]


def kernel(**inputs):
    import concourse.bacc as bacc
    from concourse.bass_utils import run_bass_kernel_spmd

    given = {k: np.asarray(x) for k, x in inputs.items()}
    laid = {k: given[k] for k in _AS_THEY_COME}
    gains, offsets = [given["ln_in_g"]], [given["ln_in_b"]]
    for i in range(DEPTH):
        gains += [given["ln1_g"][i], given["ln2_g"][i]]
        offsets += [given["ln1_b"][i], given["ln2_b"][i]]
    laid["ln"] = np.stack([np.stack(gains), np.stack(offsets)], axis=1)
    rnn = np.concatenate([given["rnn_conv_w"]] + [given[k][:, :, None] for k in
                         ("rnn_conv_b", "rg_b_a", "rg_b_x", "rg_lambda")], axis=2)
    laid["rnnp"] = rnn.reshape(DEPTH, 2, 8, KT, P).transpose(0, 4, 1, 3, 2)
    ffn = np.concatenate([given["ffn_conv_w"], given["ffn_conv_b"][:, None]], axis=1)
    laid["ffnp"] = ffn.reshape(DEPTH, 4, FF_TILES, P).transpose(0, 3, 2, 1)
    laid["rope"] = rope_tables()

    nc = bacc.Bacc("TRN2", target_bir_lowering=False, num_devices=1, dynamic_dma_scratch_size=2048)
    arrays, aps = {}, {}
    for name, x in laid.items():
        arrays[f"in_{name}_dram"] = np.ascontiguousarray(x)
        aps[name] = nc.dram_tensor(f"in_{name}_dram", x.shape, F32, kind="ExternalInput").ap()
    out = nc.dram_tensor("out_0_dram", (1, SEQ, D), F32, kind="ExternalOutput").ap()
    hybrid_encoder(nc, aps, out)
    r = run_bass_kernel_spmd(nc, [arrays], core_ids=[0])
    return r.results[0]["out_0_dram"]
```
